# Optimizing a Trainium2 kernel written in Bass

```python
import jax, jax.numpy as jnp
from jax import lax
import numpy as np

D_MODEL = 1024
BATCH = 1
SEQ = 256
DEPTH = 2

SB_HEAD_DIM = 64
SB_HEADS = D_MODEL // 128
SB_WIDTH = SB_HEADS * SB_HEAD_DIM
SB_BLOCK = 128
SSM_GROUP = 16
SSM_WIDTH = D_MODEL // 4
SSM_GROUPS = SSM_WIDTH // SSM_GROUP
SSM_STATE = 64
SSM_DT_MIN = 1e-3
SSM_DT_MAX = 1e-1
SSM_MAX_RE = -1e-4
CONV_WIDTH = D_MODEL // 4
CONV_K = 3
N_BRANCH = 3
IN_SIZES = (SB_WIDTH, SB_WIDTH, SB_WIDTH, SSM_WIDTH, CONV_WIDTH, CONV_WIDTH, CONV_WIDTH, N_BRANCH * D_MODEL)
IN_COLS = sum(IN_SIZES)
IN_SPLITS = [sum(IN_SIZES[:i + 1]) for i in range(len(IN_SIZES) - 1)]
FF_DIM = 7 * D_MODEL // 2
N_EXPERTS = 8
TOP_K = 2
N_DENSE = (DEPTH + 1) // 2
N_MOE = DEPTH // 2
EPS = 1e-6

kernel_name = 'hybrid_sb_s5_shortconv_moe_trunk'

def rms_norm(x, g):
    xf = x.astype(jnp.float32)
    y = xf * lax.rsqrt(jnp.mean(xf * xf, axis=-1, keepdims=True) + EPS)
    return (y * g.astype(jnp.float32)).astype(x.dtype)

def stick_breaking_attention(q, k, v):
    b, l, h, dh = q.shape
    nb = l // SB_BLOCK
    scale = dh ** -0.5
    kt = jnp.transpose(k, (0, 2, 1, 3))
    vt = jnp.transpose(v, (0, 2, 1, 3))
    qb = q.reshape(b, nb, SB_BLOCK, h, dh).transpose(1, 0, 3, 2, 4)
    key_pos = jnp.arange(l)

    def block(args):
        q_blk, blk = args
        z = jnp.einsum('bhqd,bhkd->bhqk', q_blk, kt).astype(jnp.float32) * scale
        q_pos = blk * SB_BLOCK + jnp.arange(SB_BLOCK)
        valid = key_pos[None, :] < q_pos[:, None]
        log_stay = jnp.where(valid, jax.nn.log_sigmoid(-z), 0.0)
        tail = lax.cumsum(log_stay, axis=3, reverse=True) - log_stay
        w = jnp.where(valid, jnp.exp(jax.nn.log_sigmoid(z) + tail), 0.0)
        return jnp.einsum('bhqk,bhkd->bhqd', w.astype(vt.dtype), vt)

    out = lax.map(block, (qb, jnp.arange(nb)))
    return out.transpose(1, 0, 3, 2, 4).reshape(b, l, h * dh)

def s5_ssm(u, lam_re, lam_im, log_dt, b_re, b_im, c_re, c_im, d_skip, w_glu):
    f32 = jnp.float32
    bsz, l, _ = u.shape
    uf = u.astype(f32)
    ug = uf.reshape(bsz, l, SSM_GROUPS, SSM_GROUP)
    lr = jnp.minimum(lam_re.astype(f32), SSM_MAX_RE)
    li = lam_im.astype(f32)
    dt = jnp.exp(log_dt.astype(f32))[:, None]
    mag = jnp.exp(lr * dt)
    ab_re = mag * jnp.cos(li * dt)
    ab_im = mag * jnp.sin(li * dt)
    den = lr * lr + li * li
    nr = ab_re - 1.0
    ni = ab_im
    f_re = (nr * lr + ni * li) / den
    f_im = (ni * lr - nr * li) / den
    br = b_re.astype(f32)
    bi = b_im.astype(f32)
    bb_re = f_re[..., None] * br - f_im[..., None] * bi
    bb_im = f_re[..., None] * bi + f_im[..., None] * br
    bu_re = jnp.einsum('gph,blgh->blgp', bb_re, ug)
    bu_im = jnp.einsum('gph,blgh->blgp', bb_im, ug)
    a_re = jnp.broadcast_to(ab_re, bu_re.shape)
    a_im = jnp.broadcast_to(ab_im, bu_im.shape)

    def combine(left, right):
        a1r, a1i, b1r, b1i = left
        a2r, a2i, b2r, b2i = right
        return (a2r * a1r - a2i * a1i, a2r * a1i + a2i * a1r,
                a2r * b1r - a2i * b1i + b2r, a2r * b1i + a2i * b1r + b2i)

    _, _, s_re, s_im = lax.associative_scan(combine, (a_re, a_im, bu_re, bu_im), axis=1)
    y = (jnp.einsum('ghp,blgp->blgh', c_re.astype(f32), s_re)
         - jnp.einsum('ghp,blgp->blgh', c_im.astype(f32), s_im))
    y = y.reshape(bsz, l, SSM_WIDTH) + d_skip.astype(f32) * uf
    y = jax.nn.gelu(y)
    y = y * jax.nn.sigmoid(y @ w_glu.astype(f32))
    return y.astype(u.dtype)

def short_conv(h, b_gate, c_gate, conv_w):
    u = c_gate * h
    y = lax.conv_general_dilated(u, conv_w[:, None, :].astype(u.dtype), window_strides=(1,),
                                 padding=((CONV_K - 1, 0),),
                                 dimension_numbers=('NWC', 'WIO', 'NWC'),
                                 feature_group_count=CONV_WIDTH)
    return b_gate * y

def hybrid_mixer(xn, w_in, lam_re, lam_im, log_dt, b_re, b_im, c_re, c_im, d_skip, w_glu,
                 conv_w, w_br_a, w_br_b, w_br_c, w_out):
    bsz, l, _ = xn.shape
    proj = xn @ w_in
    q, k, v, u_ssm, h_conv, b_gate, c_gate, gate_logits = jnp.split(proj, IN_SPLITS, axis=-1)
    heads = (bsz, l, SB_HEADS, SB_HEAD_DIM)
    y_a = stick_breaking_attention(q.reshape(heads), k.reshape(heads), v.reshape(heads)) @ w_br_a
    y_b = s5_ssm(u_ssm, lam_re, lam_im, log_dt, b_re, b_im, c_re, c_im, d_skip, w_glu) @ w_br_b
    y_c = short_conv(h_conv, b_gate, c_gate, conv_w) @ w_br_c
    g = jax.nn.sigmoid(gate_logits).reshape(bsz, l, N_BRANCH, D_MODEL)
    merged = g[:, :, 0] * y_a + g[:, :, 1] * y_b + g[:, :, 2] * y_c
    return merged @ w_out

def swiglu(x, w_gate, w_up, w_down):
    return (jax.nn.silu(x @ w_gate) * (x @ w_up)) @ w_down

def moe_swiglu(xn, w_router, w_gate, w_up, w_down):
    logits = (xn @ w_router).astype(jnp.float32)
    top_vals, top_idx = lax.top_k(logits, TOP_K)
    top_w = jax.nn.softmax(top_vals, axis=-1)
    combine = jnp.sum(jax.nn.one_hot(top_idx, N_EXPERTS, dtype=jnp.float32) * top_w[..., None], axis=-2)
    out = jnp.zeros_like(xn)
    for e in range(N_EXPERTS):
        out = out + combine[..., e:e + 1].astype(xn.dtype) * swiglu(xn, w_gate[e], w_up[e], w_down[e])
    return out

def setup_inputs(seed: int = 0) -> dict:
    key = jax.random.key(seed)
    ks = jax.random.split(key, 26)
    f32 = jnp.float32

    def nrm(k, shape, scale):
        return jax.random.normal(k, shape, f32) * scale

    def gain(k, shape):
        return 1.0 + 0.05 * jax.random.normal(k, shape, f32)

    ssm_shape = (DEPTH, SSM_GROUPS, SSM_STATE)
    n_idx = jnp.arange(SSM_STATE, dtype=f32)
    return {
        'x': nrm(ks[0], (BATCH, SEQ, D_MODEL), 1.0),
        'norm_mix': gain(ks[1], (DEPTH, D_MODEL)),
        'w_in': nrm(ks[2], (DEPTH, D_MODEL, IN_COLS), D_MODEL ** -0.5),
        'ssm_lambda_re': -0.5 + 0.01 * jax.random.normal(ks[3], ssm_shape, f32),
        'ssm_lambda_im': jnp.pi * n_idx + 0.01 * jax.random.normal(ks[4], ssm_shape, f32),
        'ssm_log_dt': jax.random.uniform(ks[5], (DEPTH, SSM_GROUPS), f32,
                                         float(np.log(SSM_DT_MIN)), float(np.log(SSM_DT_MAX))),
        'ssm_b_re': nrm(ks[6], (DEPTH, SSM_GROUPS, SSM_STATE, SSM_GROUP), (2 * SSM_GROUP) ** -0.5),
        'ssm_b_im': nrm(ks[7], (DEPTH, SSM_GROUPS, SSM_STATE, SSM_GROUP), (2 * SSM_GROUP) ** -0.5),
        'ssm_c_re': nrm(ks[8], (DEPTH, SSM_GROUPS, SSM_GROUP, SSM_STATE), SSM_STATE ** -0.5),
        'ssm_c_im': nrm(ks[9], (DEPTH, SSM_GROUPS, SSM_GROUP, SSM_STATE), SSM_STATE ** -0.5),
        'ssm_d': nrm(ks[10], (DEPTH, SSM_WIDTH), 1.0),
        'ssm_w_glu': nrm(ks[11], (DEPTH, SSM_WIDTH, SSM_WIDTH), SSM_WIDTH ** -0.5),
        'conv_w': nrm(ks[12], (DEPTH, CONV_K, CONV_WIDTH), CONV_K ** -0.5),
        'w_br_a': nrm(ks[13], (DEPTH, SB_WIDTH, D_MODEL), SB_WIDTH ** -0.5),
        'w_br_b': nrm(ks[14], (DEPTH, SSM_WIDTH, D_MODEL), SSM_WIDTH ** -0.5),
        'w_br_c': nrm(ks[15], (DEPTH, CONV_WIDTH, D_MODEL), CONV_WIDTH ** -0.5),
        'w_out': nrm(ks[16], (DEPTH, D_MODEL, D_MODEL), D_MODEL ** -0.5),
        'norm_ffn': gain(ks[17], (DEPTH, D_MODEL)),
        'dense_w_gate': nrm(ks[18], (N_DENSE, D_MODEL, FF_DIM), D_MODEL ** -0.5),
        'dense_w_up': nrm(ks[19], (N_DENSE, D_MODEL, FF_DIM), D_MODEL ** -0.5),
        'dense_w_down': nrm(ks[20], (N_DENSE, FF_DIM, D_MODEL), FF_DIM ** -0.5),
        'moe_w_router': nrm(ks[21], (N_MOE, D_MODEL, N_EXPERTS), D_MODEL ** -0.5),
        'moe_w_gate': nrm(ks[22], (N_MOE, N_EXPERTS, D_MODEL, FF_DIM), D_MODEL ** -0.5),
        'moe_w_up': nrm(ks[23], (N_MOE, N_EXPERTS, D_MODEL, FF_DIM), D_MODEL ** -0.5),
        'moe_w_down': nrm(ks[24], (N_MOE, N_EXPERTS, FF_DIM, D_MODEL), FF_DIM ** -0.5),
        'final_norm': gain(ks[25], (D_MODEL,)),
    }

def reference(x, norm_mix, w_in, ssm_lambda_re, ssm_lambda_im, ssm_log_dt, ssm_b_re, ssm_b_im,
              ssm_c_re, ssm_c_im, ssm_d, ssm_w_glu, conv_w, w_br_a, w_br_b, w_br_c, w_out,
              norm_ffn, dense_w_gate, dense_w_up, dense_w_down, moe_w_router, moe_w_gate,
              moe_w_up, moe_w_down, final_norm):
    h = x
    for i in range(DEPTH):
        xn = rms_norm(h, norm_mix[i])
        h = h + hybrid_mixer(xn, w_in[i], ssm_lambda_re[i], ssm_lambda_im[i], ssm_log_dt[i],
                             ssm_b_re[i], ssm_b_im[i], ssm_c_re[i], ssm_c_im[i], ssm_d[i],
                             ssm_w_glu[i], conv_w[i], w_br_a[i], w_br_b[i], w_br_c[i], w_out[i])
        xn = rms_norm(h, norm_ffn[i])
        if i % 2 == 0:
            j = i // 2
            h = h + swiglu(xn, dense_w_gate[j], dense_w_up[j], dense_w_down[j])
        else:
            j = i // 2
            h = h + moe_swiglu(xn, moe_w_router[j], moe_w_gate[j], moe_w_up[j], moe_w_down[j])
    return rms_norm(h, final_norm)


_drawn_inputs = setup_inputs


def setup_inputs(seed=0):
    import zlib

    import numpy as np

    out = dict(_drawn_inputs(seed))
    spreads = {}
    factors = {}
    for name, (base, spread) in spreads.items():
        noise = np.random.default_rng([zlib.crc32(name.encode()), seed]).standard_normal(out[name].shape)
        drawn = base * np.exp(spread * noise) if base else spread * noise
        out[name] = __import__('jax').numpy.asarray(drawn.astype(out[name].dtype))
    for name, factor in factors.items():
        out[name] = (out[name] * factor).astype(out[name].dtype)
    return out
```

```python
import math

import concourse.bass as bass
from concourse import mybir
from contextlib import ExitStack


def trunk_kernel(nc, x, gain_mix, w_in, lam_re, lam_im, log_dt, b_re, b_im, c_re, c_im, ssm_d, w_glu,
                 conv_w, w_br_a, w_br_b, w_br_c, w_out, gain_ffn, dense_gate, dense_up, dense_down,
                 w_router, moe_gate, moe_up, moe_down, gain_final, out):
    F32 = mybir.dt.float32
    I32 = mybir.dt.int32
    ALU = mybir.AluOpType
    ACT = mybir.ActivationFunctionType
    AX = mybir.AxisListType

    P = 128
    L = x.shape[0]
    D = x.shape[1]
    DEPTH = w_in.shape[0]
    KT = D // P
    TT = L // P
    UC = 512
    DH = 64
    QW = w_br_a.shape[1]
    HEADS = QW // DH
    HB = 4
    NB = HEADS // HB
    CW = w_br_b.shape[1]
    CT = CW // P
    GH = b_re.shape[3]
    SJ = b_re.shape[1] * b_re.shape[2] // P
    FF = dense_gate.shape[2]
    NCH = FF // UC
    FT = UC // P
    NE = w_router.shape[2]
    SLOTS = 96
    ROUNDS = -(-L // SLOTS)
    CAND = ROUNDS * NE
    EPS = 1e-6
    SCALE = DH ** -0.5
    GATE0 = 3 * QW + 4 * CW

    def cols(w, c):
        return w[:, c:c + UC].rearrange("(k p) n -> p k n", p=P)

    def rows(w):
        return w.rearrange("(k p) n -> p k n", p=P)

    MIXER = ["q", "k", "v", "uh", "bc", "gC0", "gC1", "brC", "gA0", "gA1", "brA", "gB0", "gB1", "brB",
             "wo0", "wo1"]
    FFN = ["g0", "u0"]
    for c in range(1, NCH):
        FFN += [f"g{c}", f"u{c}", f"d{c - 1}"]
    FFN += [f"d{NCH - 1}"]
    RING = 7
    LU = len(MIXER) + len(FFN)

    def unit(l, name):
        if name in MIXER:
            return l * LU + MIXER.index(name)
        return l * LU + len(MIXER) + FFN.index(name)

    GATE_OF = {"A": 0, "B": 1, "C": 2}

    def mixer_source(l, name):
        if name in ("q", "k", "v", "uh", "bc"):
            return cols(w_in[l], UC * MIXER.index(name))
        if name[0] == "g":
            return cols(w_in[l], GATE0 + GATE_OF[name[1]] * D + UC * int(name[2]))
        if name == "brA":
            return rows(w_br_a[l])
        if name == "brB":
            return rows(w_br_b[l])
        if name == "brC":
            return rows(w_br_c[l])
        return cols(w_out[l], UC * int(name[2]))

    STEPS = [("q", 0), ("q", 1), ("k", 0), ("k", 1), ("v", 0), ("v", 1), ("z", 0), ("bbT", 0),
             ("u", 0), ("softplus", 0), ("h", 0), ("b", 0), ("c", 0), ("tail", 0)]
    BU_AFTER = [0, 1, 3, 4, 6, 7, 9, 10]
    YS_AFTER = [3, 4, 6, 7, 9, 10, 12, 13]
    for t in range(2 * KT):
        STEPS.append(("gC", t) if t < KT else ("gA", t - KT))
        if t == 1:
            STEPS.append(("attend", 0))
        if t == 2:
            STEPS.append(("z", 1))
        if t == 3:
            STEPS.append(("softplus", 1))
        if t == 4:
            STEPS.append(("tail", 1))
        if t == 6:
            STEPS.append(("attend", 1))
        if t in YS_AFTER:
            STEPS.append(("ys", YS_AFTER.index(t)))
        if t in BU_AFTER:
            STEPS.append(("bu", BU_AFTER.index(t)))
        if t == 14:
            STEPS.append(("gelu", 0))
    STEPS.append(("glu", 0))
    STEPS += [("gB", t) for t in range(KT)]
    STEPS += [("wo", t) for t in range(KT)]

    GROUPS = [("in", t) for t in range(KT * TT // 4)]
    NOT_WORK = ("z", "softplus", "tail", "attend", "ys", "gelu")
    for l in range(DEPTH):
        GROUPS.append(("rms", l, 0))
        GROUPS += [(l, *s) for s in STEPS if s[0] not in NOT_WORK]
        GROUPS.append(("rms", l, 1))
        if l == 0:
            GROUPS += [("dense", t) for t in range(NCH * FT)]
    GROUPS += [("router", 0)] + [("tok", t) for t in range(4 * TT)] + [("rank", 0)]
    GROUPS += [("gather0", 0), ("gather0", 1)]
    ITEM0 = len(GROUPS)
    ITEM_GROUPS = ([("f", t) for t in range(NCH * FT)] + [("gather", 0), ("gather", 1)]
                   + [("yT", 0), ("yT", 1)] + [("comb", t) for t in range(2 * TT)])
    WB = 3
    assert len(ITEM_GROUPS) % WB == 0
    IG = len(ITEM_GROUPS)
    INDEX = {g: n for n, g in enumerate(GROUPS)}
    ITEM_INDEX = {g: n for n, g in enumerate(ITEM_GROUPS)}

    class Group:

        def __init__(self, key, item=None):
            n = INDEX[key] if item is None else ITEM0 + ITEM_INDEX[key]
            self.n = n
            self.bank = n % WB
            self.done = n + 1 if item is None else item * IG + (n + 1)

    ctx = ExitStack()
    with ctx:
        def sb(name, shape, dt=F32):
            return ctx.enter_context(nc.sbuf_tensor(name, shape, dt))

        def sem(name):
            return ctx.enter_context(nc.semaphore(name))

        ring = sb("ring", [P, RING, KT * UC])
        hT = sb("hT", [P, KT, L])
        xnT = sb("xnT", [P, KT, L])
        ident = sb("ident", [P, P])
        neg_incl = sb("neg_incl", [P, P])
        neg_ones = sb("neg_ones", [P, P])
        rstd = sb("rstd", [P, L])
        gains = sb("gains", [P, 2 * DEPTH, KT])
        lam = sb("lam", [P, 2, DEPTH * SJ])
        logdt = sb("logdt", [P, DEPTH * SJ])
        bias = sb("bias", [P, 2])
        slot_no = sb("slot_no", [P, SLOTS])
        dskip = sb("dskip", [P, DEPTH, CT])
        convw = sb("convw", [P, DEPTH, 3, CT])
        small = sb("small", [P, 16, DEPTH * SJ])
        (dt, lr, decay, angle, mag, turns, reduced, upright, sin1, cos1, den, tmp1, nr, tmp2, f_re,
         f_im) = [small[:, n, :] for n in range(16)]
        power = sb("power", [P, 5, SJ])
        wr = sb("wr", [P, KT, NE])
        wglu = sb("wglu", [P, CT, CW])
        cblk = sb("cblk", [P, 2, SJ, 2 * GH])
        bbT = sb("bbT", [P, 4, P])
        sig = sb("sig", [P, 2, L])
        ARENA = 16392
        arena = sb("arena", [P, ARENA])
        at = [0]

        def carve(n):
            at[0] += n
            assert at[0] <= ARENA, at[0]
            return arena[:, at[0] - n:at[0]]

        qT = carve(QW // P * L).rearrange("p (t n) -> p t n", n=L)
        kT = carve(QW // P * L).rearrange("p (t n) -> p t n", n=L)
        v = carve(TT * QW).rearrange("p (t n) -> p t n", n=QW)
        AW = L + P
        attn = carve(HB * AW).rearrange("p (h n) -> p h n", n=AW)
        uT = carve(CT * L).rearrange("p (t n) -> p t n", n=L)
        hconv = carve(CT * L).rearrange("p (t n) -> p t n", n=L)
        bconv = carve(CT * L).rearrange("p (t n) -> p t n", n=L)
        uconv = carve(CT * (L + 2)).rearrange("p (t n) -> p t n", n=L + 2)
        cosT = carve(SJ * L).rearrange("p (j n) -> p j n", n=L)
        sinT = carve(SJ * L).rearrange("p (j n) -> p j n", n=L)
        vtmp = carve(2 * L).rearrange("p (t n) -> p t n", n=L)
        rtmp = carve(4 * L).rearrange("p (t n) -> p t n", n=L)
        sring = carve(4 * 2 * L).rearrange("p (t c n) -> p t c n", c=2, n=L)
        bbp = sring[:, 3, :, :]
        braw = sring[:, 2, 0, 0:2 * SJ * GH].rearrange("p (c j h) -> p c j h", c=2, h=GH)
        craw = sring[:, 2, 1, 0:2 * SJ * GH].rearrange("p (c j h) -> p c j h", c=2, h=GH)
        merged = carve(KT * L).rearrange("p (t n) -> p t n", n=L)
        x_in = arena[:, 0:TT * D].rearrange("p (t n) -> p t n", n=D)
        at[0] = 0
        hid = carve(2 * FT * L).rearrange("p (b t n) -> p b t n", b=2, n=L)
        at[0] = 0
        ehid = carve(2 * FT * SLOTS).rearrange("p (b t n) -> p b t n", b=2, n=SLOTS)
        h_tok = carve(TT * D).rearrange("p (t n) -> p t n", n=D)
        xn_tok = carve(TT * D).rearrange("p (t n) -> p t n", n=D)
        xe = carve(KT * SLOTS).rearrange("p (t n) -> p t n", n=SLOTS)
        yT = carve(KT * SLOTS).rearrange("p (t n) -> p t n", n=SLOTS)
        y_tok = carve(D)
        pick = carve(TT * SLOTS).rearrange("p (t n) -> p t n", n=SLOTS)
        wpick = carve(TT * SLOTS).rearrange("p (t n) -> p t n", n=SLOTS)
        combine = carve(L)
        g_row = carve(D)
        rank_c = carve(TT * CAND).rearrange("p (t n) -> p t n", n=CAND)
        wgt_c = carve(TT * CAND).rearrange("p (t n) -> p t n", n=CAND)
        logits = carve(TT * NE).rearrange("p (t n) -> p t n", n=NE)
        mask1 = carve(TT * NE).rearrange("p (t n) -> p t n", n=NE)
        mask2 = carve(TT * NE).rearrange("p (t n) -> p t n", n=NE)
        chosen = carve(TT * NE).rearrange("p (t n) -> p t n", n=NE)
        rest = carve(TT * NE).rearrange("p (t n) -> p t n", n=NE)
        order = carve(TT * NE).rearrange("p (t n) -> p t n", n=NE)
        stat = carve(TT * 8).rearrange("p (t n) -> p t n", n=8)
        XC = CAND - NE
        active = carve(XC)
        place = carve(XC)
        value = carve(XC)
        grid = carve(XC * XC).rearrange("p (i c) -> p i c", c=XC)
        counts = carve(NE)
        listf = carve(CAND + 2)
        neg_rank = carve((TT + 1) * NE).rearrange("p (t n) -> p t n", n=NE)
        sumsq = carve(TT)
        out_tile = xn_tok
        items = sb("items", [P, CAND + 2], I32)

        acc = ctx.enter_context(nc.psum_tensor("acc", [P, 4, 512], F32))
        ssm_y = ctx.enter_context(nc.psum_tensor("ssm_y", [P, CT, L], F32))
        work = ctx.enter_context(nc.psum_tensor("work", [P, WB, 512], F32))
        attn_z = acc[:, :, 0:AW]

        slot_full = [sem(f"slot_full{n}") for n in range(RING)]
        work_done = sem("work_done")
        x_loaded = sem("x_loaded")
        params_loaded = sem("params_loaded")
        ssm_loaded = sem("ssm_loaded")
        glu_loaded = sem("glu_loaded")
        wr_loaded = sem("wr_loaded")
        row_loaded = sem("row_loaded")
        consts_made = sem("consts_made")
        h_ready = sem("h_ready")
        sq_ready = sem("sq_ready")
        rstd_ready = sem("rstd_ready")
        xn_ready = sem("xn_ready")
        q_ready = sem("q_ready")
        k_ready = sem("k_ready")
        v_ready = sem("v_ready")
        z_done = sem("z_done")
        log_ready = sem("log_ready")
        stay_ready = sem("stay_ready")
        stay_masked = sem("stay_masked")
        tail_done = sem("tail_done")
        w_ready = sem("w_ready")
        w_masked = sem("w_masked")
        attn_done = sem("attn_done")
        attn_read = sem("attn_read")
        h_conv_ready = sem("h_conv_ready")
        b_conv_ready = sem("b_conv_ready")
        conv_ready = sem("conv_ready")
        u_ready = sem("u_ready")
        dt_ready = sem("dt_ready")
        angle_ready = sem("angle_ready")
        sincos_ready = sem("sincos_ready")
        f_ready = sem("f_ready")
        bbp_ready = sem("bbp_ready")
        bbT_ready = sem("bbT_ready")
        c_ready = sem("c_ready")
        tables_ready = sem("tables_ready")
        scanned = sem("scanned")
        states_ready = sem("states_ready")
        states_used = sem("states_used")
        gelu_in = sem("gelu_in")
        gelu_out = sem("gelu_out")
        glu_ready = sem("glu_ready")
        yb_ready = sem("yb_ready")
        sig_ready = sem("sig_ready")
        merged_ready = sem("merged_ready")
        silu_ready = sem("silu_ready")
        hid_ready = sem("hid_ready")
        down_chunk = sem("down_chunk")
        logits_ready = sem("logits_ready")
        chosen_ready = sem("chosen_ready")
        tok_ready = sem("tok_ready")
        items_ready = sem("items_ready")
        pick_ready = sem("pick_ready")
        wpick_turned = sem("wpick_turned")
        combine_ready = sem("combine_ready")
        xe_ready = sem("xe_ready")
        yT_ready = sem("yT_ready")
        y_ready = sem("y_ready")
        rms_read = sem("rms_read")
        conv_u_ready = sem("conv_u_ready")
        bu_read = sem("bu_read")
        gate_used = sem("gate_used")
        rank_read = sem("rank_read")
        diff_ready = sem("diff_ready")
        expd_ready = sem("expd_ready")
        h_tok_ready = sem("h_tok_ready")
        sumsq_ready = sem("sumsq_ready")
        final_rstd = sem("final_rstd")
        rows_ready = sem("rows_ready")
        out_stored = sem("out_stored")
        act_chain = sem("act_chain")
        dve_chain = sem("dve_chain")
        pool_chain = sem("pool_chain")

        block = ctx.enter_context(nc.Block())
        FFN_TILES = NCH * FT
        IN_BANKS = KT * TT // 4
        H_MIXED = [IN_BANKS, IN_BANKS + KT + 4]
        GATES = ["C", "A", "B"]

        def gate_number(l, branch, t):
            return (l * len(GATES) + GATES.index(branch)) * KT + t

        def reader(key, item=None):
            kind = key[0]
            if item is not None:
                t = key[1]
                return {"f": (hid_ready, item * FFN_TILES + (FFN_TILES + t + 1)),
                        "gather": (xe_ready, item * 2 + (3 + t)),
                        "yT": (y_ready, item * 2 + (1 + t)),
                        "comb": (h_tok_ready, item * 2 * TT + (2 * TT + t + 1))}[kind]
            if kind == "in":
                return h_ready, key[1] + 1
            if kind == "rms":
                return rms_read, 2 * key[1] + key[2] + 1
            if kind == "dense":
                return hid_ready, key[1] + 1
            if kind == "router":
                return logits_ready, 1
            if kind == "tok":
                return (tok_ready, key[1] + 1) if key[1] < 2 * TT else (h_tok_ready, key[1] - 2 * TT + 1)
            if kind == "rank":
                return rank_read, 1
            if kind == "gather0":
                return xe_ready, key[1] + 1
            l, kind, t = key
            if kind[0] == "g" and kind[1:] in GATES:
                return gate_used, gate_number(l, kind[1], t) + 1
            return {"q": (q_ready, 2 * l + t + 1), "k": (k_ready, 2 * l + t + 1), "v": (v_ready, 2 * l + t + 1),
                    "bbT": (bbT_ready, l + 1), "u": (u_ready, l + 1), "h": (h_conv_ready, l + 1),
                    "b": (b_conv_ready, l + 1), "c": (conv_u_ready, l + 1), "bu": (bu_read, l * SJ + t + 1),
                    "glu": (glu_ready, l + 1), "wo": (h_ready, H_MIXED[l] + t + 1)}[kind]
        D_UNITS = len(FFN)
        PARAMS = 2 + 2 + 2 * DEPTH + 2
        HALF = KT // 2

        def slot(n):
            return n % RING

        def slot_view(name, n):
            s = ring[:, slot(n), :]
            if name[0] == "d" or name.startswith("br"):
                k = {"brA": QW // P, "brB": CT, "brC": CT}.get(name, FT)
                return s[:, 0:k * D].rearrange("p (k n) -> p k n", n=D)
            return s.rearrange("p (k n) -> p k n", n=UC)

        @block.sync
        def _(sp):
            sp.dma_start(x_in[:, :, :], x.rearrange("(t p) d -> p t d", p=P)).then_inc(x_loaded, 16)

            def await_release(l, name, item=None):
                if name[0] == "d":
                    c = NCH * l + int(name[1]) + 1
                    sp.wait_ge(down_chunk, c if item is None else item * NCH + c)
                    return
                if name in ("g%d" % c for c in range(NCH)) or name in ("u%d" % c for c in range(NCH)):
                    last = ("dense" if l == 0 else "f", int(name[1]) * FT + FT - 1)
                    sp.wait_ge(work_done, Group(last, item).done)
                    return
                kind, t = {"q": ("q", 1), "k": ("k", 1), "v": ("v", 1), "uh": ("h", 0), "bc": ("c", 0),
                           "wo0": ("wo", 3), "wo1": ("wo", 7), "brA": ("gA", 7), "brB": ("gB", 7),
                           "brC": ("gC", 7)}.get(name) or (name[0:2], 4 * int(name[2]) + 3)
                sp.wait_ge(work_done, Group((l, kind, t)).done)

            def load(l, name, source, item=None, before=None):
                n = unit(l, name)
                if before is not None:
                    await_release(*before)
                elif n >= RING:
                    m = n - RING
                    await_release(m // LU, (MIXER + FFN)[m % LU])
                sp.dma_start(slot_view(name, n), source).then_inc(slot_full[slot(n)], 16)

            for l in range(DEPTH):
                for name in MIXER:
                    load(l, name, mixer_source(l, name))
                if l == 0:
                    for name in FFN:
                        c = int(name[1])
                        src = {"g": dense_gate, "u": dense_up, "d": dense_down}[name[0]][0]
                        load(0, name, rows(src[UC * c:UC * c + UC, :]) if name[0] == "d" else cols(src, UC * c))

            def expert(i, e, first=False):
                for u, name in enumerate(FFN):
                    c = int(name[1])
                    src = {"g": moe_gate, "u": moe_up, "d": moe_down}[name[0]]
                    w = src[0, bass.ds(e, 1), :, :].rearrange("a k n -> (a k) n")
                    if u >= RING:
                        before = (1, FFN[u - RING], i)
                    else:
                        before = None if first else (1, FFN[u - RING], i - 1)
                    load(1, name, rows(w[UC * c:UC * c + UC, :]) if name[0] == "d" else cols(w, UC * c),
                         item=i, before=before)

            expert(0, 0, first=True)
            with sp.Fori(1, NE) as i:
                expert(i, i)
            sp.wait_ge(items_ready, 1)
            n_items = sp.value_load(items[0:1, CAND + 1:CAND + 2], min_val=NE, max_val=CAND)
            with sp.If(n_items > NE):
                with sp.Fori(NE, n_items) as i:
                    c = sp.value_load(items[0:1, bass.ds(i, 1)], min_val=0, max_val=CAND - 1)
                    expert(i, c % NE)
            sp.wait_ge(rows_ready, TT)
            sp.dma_start(out.rearrange("(t p) d -> p t d", p=P), out_tile[:, :, :]).then_inc(out_stored, 16)
            sp.wait_ge(out_stored, 16)

        @block.tensor
        def _(pe):
            def begin(g, item=None):
                n = g.n - WB
                if item is None:
                    if n >= 0:
                        pe.wait_ge(*reader(GROUPS[n]))
                elif n >= ITEM0:
                    pe.wait_ge(*reader(ITEM_GROUPS[n - ITEM0], item))
                else:
                    t = ITEM_GROUPS[n - ITEM0 + IG][1]
                    pe.wait_ge(h_tok_ready, item * 2 * TT + (t + 1))
                return work[:, g.bank, :]

            def weights(l, name, item=None):
                n = unit(l, name)
                if item is None:
                    pe.wait_ge(slot_full[slot(n)], 16 * (n // RING + 1))
                else:
                    pe.wait_ge(slot_full[slot(n)], item * (16 * D_UNITS // RING) + 16 * (n // RING + 1))
                return slot_view(name, n)

            def accumulate(out_ap, pairs, start=True, stop=True, shared=False):
                for n, (a, b) in enumerate(pairs):
                    last = nc.tensor.matmul(out_ap, a, b, start=start and n == 0,
                                            stop=stop and n == len(pairs) - 1, skip_group_check=shared)
                return last

            def sum_squares(l, part):
                g = Group(("rms", l, part))
                bank = begin(g)
                for k in range(KT):
                    pe.wait_ge(sq_ready, (2 * l + part) * KT + k + 1)
                    last = nc.tensor.matmul(bank[:, 0:L], neg_ones[:, :], xnT[:, k, :], start=k == 0,
                                            stop=k == KT - 1)
                last.then_inc(work_done, 1)

            pe.wait_ge(consts_made, 4)
            pe.wait_ge(x_loaded, 16)
            for t in range(KT * TT // 4):
                g = Group(("in", t))
                bank = begin(g)
                for q in range(4):
                    k, tt = (4 * t + q) // TT, (4 * t + q) % TT
                    last = nc.tensor.transpose(bank[:, q * P:q * P + P], x_in[:, tt, k * P:k * P + P],
                                               ident[:, :])
                last.then_inc(work_done, 1)

            for l in range(DEPTH):
                sum_squares(l, 0)
                pe.wait_ge(xn_ready, (2 * l + 1) * KT)
                for kind, t in STEPS:
                    if kind in ("gelu", "softplus"):
                        continue
                    g = None if kind in NOT_WORK else Group((l, kind, t))
                    bank = None if g is None else begin(g)
                    if kind in ("q", "k", "u", "h", "b", "c"):
                        name = {"q": "q", "k": "k", "u": "uh", "h": "uh", "b": "bc", "c": "bc"}[kind]
                        first = {"q": 2 * t, "k": 2 * t, "u": 0, "h": 2, "b": 0, "c": 2}[kind]
                        w = weights(l, name)
                        for q in range(2):
                            last = accumulate(bank[:, q * L:q * L + L],
                                              [(w[:, k, (first + q) * P:(first + q + 1) * P], xnT[:, k, :])
                                               for k in range(KT)])
                        last.then_inc(work_done, 1)
                    elif kind == "v":
                        w = weights(l, "v")
                        last = accumulate(bank[:, :], [(xnT[:, k, t * P:t * P + P], w[:, k, :])
                                                       for k in range(KT)])
                        last.then_inc(work_done, 1)
                    elif kind == "z":
                        pe.wait_ge(q_ready, 2 * l + t + 1)
                        pe.wait_ge(k_ready, 2 * l + t + 1)
                        if 2 * l + t:
                            pe.wait_ge(attn_read, 2 * l + t)
                        for n in range(HB):
                            h = t * HB + n
                            r = slice(DH * (h % 2), DH * (h % 2) + DH)
                            nc.tensor.matmul(acc[:, n, 0:L], kT[r, h // 2, 0:P], qT[r, h // 2, :],
                                             start=True, stop=True, skip_group_check=True)
                            last = nc.tensor.matmul(acc[:, n, L:AW], kT[r, h // 2, P:L], qT[r, h // 2, P:L],
                                                    start=False, stop=True, skip_group_check=True)
                        last.then_inc(z_done, 1)
                    elif kind == "tail":
                        pe.wait_ge(stay_masked, 2 * l + t + 1)
                        for n in range(HB):
                            nc.tensor.matmul(acc[:, n, 0:AW], neg_incl[:, :], attn[:, n, :],
                                             start=False, stop=True, skip_group_check=True)
                            last = nc.tensor.matmul(acc[:, n, P:L], neg_ones[:, :], attn[:, n, L:AW],
                                                    start=False, stop=True, skip_group_check=True)
                        last.then_inc(tail_done, 1)
                    elif kind == "attend":
                        pe.wait_ge(w_masked, 2 * l + t + 1)
                        if t == 0:
                            pe.wait_ge(v_ready, 2 * l + 2)
                        for n in range(HB):
                            h = t * HB + n
                            r = slice(DH * (h % 2), DH * (h % 2) + DH)
                            hc = slice(h * DH, h * DH + DH)
                            nc.tensor.matmul(acc[r, n // 2, 0:L], v[:, 0, hc], attn[:, n, 0:L],
                                             start=True, stop=False, skip_group_check=True)
                            last = nc.tensor.matmul(acc[r, n // 2, P:L], v[:, 1, hc], attn[:, n, L:AW],
                                                    start=False, stop=True, skip_group_check=True)
                        last.then_inc(attn_done, 1)
                    elif kind == "bbT":
                        pe.wait_ge(bbp_ready, l + 1)
                        for q in range(4):
                            last = nc.tensor.transpose(bank[:, q * P:q * P + P],
                                                       bbp[:, q // 2, (q % 2) * P:(q % 2) * P + P], ident[:, :])
                        last.then_inc(work_done, 1)
                    elif kind == "bu":
                        if t == 0:
                            pe.wait_ge(bbT_ready, l + 1)
                            pe.wait_ge(u_ready, l + 1)
                        a, b = t // 4, 32 * (t % 4)
                        for q in range(2):
                            last = nc.tensor.matmul(bank[:, q * L:q * L + L], bbT[b:b + 32, 2 * q + a, :],
                                                    uT[b:b + 32, a, :], start=True, stop=True)
                        last.then_inc(work_done, 1)
                    elif kind == "ys":
                        pe.wait_ge(states_ready, l * SJ + t + 1)
                        if t == 0:
                            pe.wait_ge(c_ready, l + 1)
                        a, b = t // 4, 32 * (t % 4)
                        for q in range(2):
                            last = nc.tensor.matmul(ssm_y[b:b + 32, a, :], cblk[:, q, t, :], sring[:, t % 4, q, :],
                                                    start=q == 0, stop=q == 1)
                        last.then_inc(states_used, 1)
                    elif kind == "glu":
                        pe.wait_ge(glu_loaded, 16 * (l + 1))
                        pe.wait_ge(gelu_out, CT * (l + 1))
                        for q in range(CT):
                            last = accumulate(bank[:, q * L:q * L + L],
                                              [(wglu[:, k, q * P:q * P + P], uT[:, k, :]) for k in range(CT)])
                        last.then_inc(work_done, 1)
                    elif kind[0] == "g":
                        br = kind[1]
                        w = weights(l, f"{kind}{t // 4}")
                        accumulate(bank[:, 0:L], [(w[:, k, (t % 4) * P:(t % 4) * P + P], xnT[:, k, :])
                                                  for k in range(KT)])
                        if t == 0:
                            if br == "C":
                                pe.wait_ge(conv_ready, l + 1)
                            if br == "A":
                                pe.wait_ge(attn_read, 2 * l + 2)
                            if br == "B":
                                pe.wait_ge(yb_ready, l + 1)
                        w = weights(l, "br" + br)
                        act_in = {"A": qT, "B": uT, "C": hconv}[br]
                        kk = {"A": QW // P, "B": CT, "C": CT}[br]
                        accumulate(bank[:, L:2 * L], [(w[:, k, t * P:t * P + P], act_in[:, k, :])
                                                      for k in range(kk)]).then_inc(work_done, 1)
                    elif kind == "wo":
                        pe.wait_ge(merged_ready, (l + 1) * KT)
                        w = weights(l, f"wo{t // 4}")
                        accumulate(bank[:, 0:L], [(w[:, k, (t % 4) * P:(t % 4) * P + P], merged[:, k, :])
                                                  for k in range(KT)]).then_inc(work_done, 1)

                sum_squares(l, 1)
                pe.wait_ge(xn_ready, (2 * l + 2) * KT)

                def ffn(l, key, item, moving, width, hidden, chunk0, read_before):
                    def down(c):
                        w = weights(l, f"d{c}", item)
                        pe.wait_ge(hid_ready, chunk0 + (c + 1) * FT)
                        per = 2 if item is None else HALF
                        for f in range(FT):
                            for n in range(KT):
                                b, o = n // per, (n % per) * width
                                last = nc.tensor.matmul(acc[:, b, o:o + width], w[:, f, n * P:n * P + P],
                                                        hidden[:, c % 2, f, :],
                                                        start=c == 0 and f == 0 and n % per == 0,
                                                        stop=c == NCH - 1 and f == FT - 1,
                                                        skip_group_check=True)
                        last.then_inc(down_chunk, 1)

                    for c in range(NCH):
                        wg, wu = weights(l, f"g{c}", item), weights(l, f"u{c}", item)
                        for f in range(FT):
                            bank = begin(Group((key, c * FT + f), item), item)
                            fc = slice(f * P, f * P + P)
                            accumulate(bank[:, 0:width], [(wg[:, k, fc], moving[:, k, :]) for k in range(KT)])
                            last = accumulate(bank[:, width:2 * width], [(wu[:, k, fc], moving[:, k, :])
                                                                         for k in range(KT)])
                            last.then_inc(work_done, 1)
                        if c == 0:
                            read_before()
                        else:
                            down(c - 1)
                    down(NCH - 1)

                if l == 0:
                    ffn(0, "dense", None, xnT, L, hid, 0, lambda: None)

            bank = begin(Group(("router", 0)))
            pe.wait_ge(wr_loaded, 16)
            for t in range(TT):
                last = accumulate(bank[:, t * NE:t * NE + NE], [(xnT[:, k, t * P:t * P + P], wr[:, k, :])
                                                                for k in range(KT)])
            last.then_inc(work_done, 1)
            for t in range(4 * TT):
                bank = begin(Group(("tok", t)))
                src = xnT if t < 2 * TT else hT
                tt, half = (t % (2 * TT)) // 2, t % 2
                for q in range(4):
                    last = nc.tensor.transpose(bank[:, q * P:q * P + P],
                                               src[:, half * 4 + q, tt * P:tt * P + P], ident[:, :])
                last.then_inc(work_done, 1)
            bank = begin(Group(("rank", 0)))
            pe.wait_ge(chosen_ready, 1)
            for t in range(TT):
                pairs = [(neg_ones[:, :], chosen[:, s, :]) for s in range(t)]
                accumulate(bank[:, t * NE:t * NE + NE], pairs + [(neg_incl[:, :], rest[:, t, :]),
                                                                 (neg_ones[:, :], chosen[:, t, :])])
            accumulate(bank[:, TT * NE:TT * NE + NE], [(neg_ones[:, :], chosen[:, t, :]) for t in range(TT)])\
                .then_inc(work_done, 1)

            def gather(key, item, need):
                pe.wait_ge(pick_ready, need)
                for half in range(2):
                    bank = begin(Group((key, half), item), item)
                    for q in range(HALF):
                        d = (half * HALF + q) * P
                        last = accumulate(bank[:, q * SLOTS:q * SLOTS + SLOTS],
                                          [(xn_tok[:, t, d:d + P], pick[:, t, :]) for t in range(TT)])
                    last.then_inc(work_done, 1)

            pe.wait_ge(tok_ready, 2 * TT)
            gather("gather0", None, 1)
            pe.wait_ge(items_ready, 1)
            n_items = pe.value_load(items[0:1, CAND + 1:CAND + 2], min_val=NE, max_val=CAND)
            with pe.Fori(0, n_items) as i:
                pe.wait_ge(xe_ready, i * 2 + 2)

                def turn_weights():
                    for t in range(TT):
                        last = nc.tensor.transpose(acc[0:SLOTS, 2, t * P:t * P + P], wpick[:, t, :], ident[:, :])
                    last.then_inc(wpick_turned, 1)

                ffn(1, "f", i, xe, SLOTS, ehid, i * FFN_TILES + FFN_TILES, turn_weights)
                gather("gather", i, i + 2)
                pe.wait_ge(yT_ready, i * 2 + 2)
                for half in range(2):
                    bank = begin(Group(("yT", half), i), i)
                    for q in range(HALF):
                        last = nc.tensor.transpose(bank[0:SLOTS, q * P:q * P + P], yT[:, half * HALF + q, :],
                                                   ident[:, :])
                    last.then_inc(work_done, 1)
                pe.wait_ge(y_ready, i * 2 + 2)
                pe.wait_ge(combine_ready, i + 1)
                for t in range(2 * TT):
                    bank = begin(Group(("comb", t), i), i)
                    tt, half = t // 2, t % 2
                    nc.tensor.matmul(bank[:, :], combine[0:SLOTS, tt * P:tt * P + P],
                                     y_tok[0:SLOTS, half * 512:half * 512 + 512], start=True, stop=True)\
                        .then_inc(work_done, 1)

        @block.scalar
        def _(act):
            chain = [0]

            def link(ins):
                chain[0] += 1
                ins.then_inc(act_chain, 1)
                act.wait_ge(act_chain, chain[0])

            def arrived(g):
                act.wait_ge(work_done, g.done)
                return work[:, g.bank, :]

            act.dma_start(lam[:, 0, :], lam_re.rearrange("p l j -> p (l j)")).then_inc(params_loaded, 16)
            act.dma_start(lam[:, 1, :], lam_im.rearrange("p l j -> p (l j)")).then_inc(params_loaded, 16)
            for par in range(2):
                src = log_dt[par:par + 1].rearrange("q l j -> q (l j)").to_broadcast([P // 2, DEPTH * SJ])
                act.dma_start(logdt[par * (P // 2):par * (P // 2) + P // 2, :], src).then_inc(params_loaded, 16)
            for l in range(DEPTH):
                act.dma_start(gains[:, 2 * l, :], gain_mix[l]).then_inc(params_loaded, 16)
                act.dma_start(gains[:, 2 * l + 1, :], gain_ffn[l]).then_inc(params_loaded, 16)
            act.dma_start(dskip[:, :, :], ssm_d).then_inc(params_loaded, 16)
            act.dma_start(convw[:, :, :, :], conv_w).then_inc(params_loaded, 16)
            act.dma_start(wr[:, :, :], rows(w_router[0])).then_inc(wr_loaded, 16)

            def squares(l, part):
                for k in range(KT):
                    if part == 1:
                        act.wait_ge(h_ready, H_MIXED[l] + k + 1)
                    else:
                        act.wait_ge(h_ready, H_MIXED[l] - 4 + k // 2 + 1)
                    nc.scalar.activation(xnT[:, k, :], hT[:, k, :], ACT.Square).then_inc(sq_ready, 1)

            def root_mean_square(l, part):
                bank = arrived(Group(("rms", l, part)))
                nc.scalar.activation(rstd[:, :], bank[:, 0:L], ACT.Ln, bias=bias[:, 0:1], scale=-1.0 / D)\
                    .then_inc(rms_read, 1)
                act.wait_ge(rms_read, 2 * l + part + 1)
                nc.scalar.activation(rstd[:, :], rstd[:, :], ACT.Exp, scale=-0.5).then_inc(rstd_ready, 1)

            act.wait_ge(consts_made, 4)
            act.preload_act_table_set("natural_log_exp_and_others")
            squares(0, 0)
            root_mean_square(0, 0)
            act.wait_ge(params_loaded, 16 * PARAMS)
            nc.scalar.activation(dt, logdt[:, :], ACT.Exp).then_inc(dt_ready, 1)
            act.wait_ge(angle_ready, 1)
            nc.scalar.activation(mag, decay, ACT.Exp).then_inc(sincos_ready, 1)
            nc.scalar.activation(sin1, reduced, ACT.Sin).then_inc(sincos_ready, 1)
            nc.scalar.activation(cos1, upright, ACT.Sin).then_inc(sincos_ready, 1)
            act.preload_act_table_set("natural_log_exp_and_others")

            for l in range(DEPTH):
                if l:
                    squares(l, 0)
                    root_mean_square(l, 0)
                for kind, t in STEPS:
                    if kind == "q":
                        bank = arrived(Group((l, kind, t)))
                        nc.scalar.activation(qT[:, 2 * t:2 * t + 2, :].rearrange("p t n -> p (t n)"), bank[:, :],
                                             ACT.Copy, scale=SCALE).then_inc(q_ready, 1)
                    elif kind in ("h", "b"):
                        bank = arrived(Group((l, kind, t)))
                        dst = hconv if kind == "h" else bconv
                        nc.scalar.activation(dst[:, :, :].rearrange("p t n -> p (t n)"), bank[:, :], ACT.Copy)\
                            .then_inc(h_conv_ready if kind == "h" else b_conv_ready, 1)
                    elif kind == "bbT":
                        bank = arrived(Group((l, kind, t)))
                        nc.scalar.activation(bbT[:, :, :].rearrange("p t n -> p (t n)"), bank[:, :], ACT.Copy)\
                            .then_inc(bbT_ready, 1)
                    elif kind == "z":
                        act.wait_ge(z_done, 2 * l + t + 1)
                        link(nc.scalar.activation(attn[:, :, :], attn_z, ACT.Abs))
                        act.preload_act_table_set("natural_log_exp_and_others")
                        link(nc.scalar.activation(attn[:, :, :], attn[:, :, :], ACT.Exp, scale=-1.0))
                        nc.scalar.activation(attn[:, :, :], attn[:, :, :], ACT.Ln, bias=bias[:, 1:2])\
                            .then_inc(log_ready, 1)
                    elif kind == "tail":
                        act.wait_ge(tail_done, 2 * l + t + 1)
                        nc.scalar.activation(attn[:, :, :], attn_z, ACT.Exp).then_inc(w_ready, 1)
                    elif kind == "gelu":
                        for a in range(CT):
                            act.wait_ge(gelu_in, CT * l + a + 1)
                            nc.scalar.activation(uT[:, a, :], uT[:, a, :], ACT.Gelu_apprx_tanh)\
                                .then_inc(gelu_out, 1)
                    elif kind == "glu":
                        bank = arrived(Group((l, kind, t)))
                        nc.scalar.activation(bconv[:, :, :].rearrange("p t n -> p (t n)"), bank[:, :],
                                             ACT.Sigmoid).then_inc(glu_ready, 1)
                    elif kind in ("gA", "gB", "gC"):
                        n = gate_number(l, kind[1], t)
                        bank = arrived(Group((l, kind, t)))
                        if n >= 2:
                            act.wait_ge(gate_used, n - 1)
                        nc.scalar.activation(sig[:, n % 2, :], bank[:, 0:L], ACT.Sigmoid).then_inc(sig_ready, 1)
                act.preload_act_table_set("natural_log_exp_and_others")
                squares(l, 1)
                root_mean_square(l, 1)
                if l == 0:
                    for n in range(FFN_TILES):
                        bank = arrived(Group(("dense", n)))
                        if n >= 2:
                            act.wait_ge(hid_ready, n - 1)
                        nc.scalar.activation(sig[:, n % 2, :], bank[:, 0:L], ACT.Silu).then_inc(silu_ready, 1)

            act.dma_start(g_row, gain_final[0:1, :].to_broadcast([P, D])).then_inc(row_loaded, 16)
            for t in range(2 * TT):
                bank = arrived(Group(("tok", t)))
                nc.scalar.activation(xn_tok[:, t // 2, (t % 2) * 512:(t % 2) * 512 + 512], bank[:, :], ACT.Copy)\
                    .then_inc(tok_ready, 1)
            act.wait_ge(diff_ready, 1)
            nc.scalar.activation(stat[:, :, 3:4], stat[:, :, 2:3], ACT.Exp).then_inc(expd_ready, 1)

            def move_tokens(key, item, half):
                bank = arrived(Group((key, half), item))
                nc.scalar.activation(xe[:, half * HALF:half * HALF + HALF, :].rearrange("p t n -> p (t n)"),
                                     bank[:, 0:HALF * SLOTS], ACT.Copy).then_inc(xe_ready, 1)

            for half in range(2):
                move_tokens("gather0", None, half)
            act.wait_ge(items_ready, 1)
            n_items = act.value_load(items[0:1, CAND + 1:CAND + 2], min_val=NE, max_val=CAND)
            act.preload_act_table(ACT.Silu)
            with act.Fori(0, n_items) as i:
                for n in range(FFN_TILES):
                    if n == FT:
                        act.wait_ge(wpick_turned, i + 1)
                        nc.scalar.activation(combine[0:SLOTS, :], acc[0:SLOTS, 2, 0:L], ACT.Copy)\
                            .then_inc(combine_ready, 1)
                    bank = arrived(Group(("f", n), i))
                    act.wait_ge(hid_ready, i * FFN_TILES + (FFN_TILES + n - 1))
                    nc.scalar.activation(sig[:, n % 2, 0:SLOTS], bank[:, 0:SLOTS], ACT.Silu)\
                        .then_inc(silu_ready, 1)
                for half in range(2):
                    move_tokens("gather", i, half)
                for half in range(2):
                    bank = arrived(Group(("yT", half), i))
                    nc.scalar.activation(y_tok[0:SLOTS, half * 512:half * 512 + 512], bank[0:SLOTS, :], ACT.Copy)\
                        .then_inc(y_ready, 1)
            act.preload_act_table_set("natural_log_exp_and_others")
            act.wait_ge(h_tok_ready, n_items * 2 * TT + 2 * TT)
            for t in range(TT):
                last = nc.scalar.activation(xn_tok[:, t, :], h_tok[:, t, :], ACT.Square,
                                            accum_out=sumsq[:, t:t + 1])
                link(last)
            link(nc.scalar.activation(sumsq[:, :], sumsq[:, :], ACT.Ln, bias=bias[:, 0:1], scale=1.0 / D))
            nc.scalar.activation(sumsq[:, :], sumsq[:, :], ACT.Exp, scale=-0.5).then_inc(final_rstd, 1)

        @block.vector
        def _(dve):
            chain = [0]

            def link(ins):
                chain[0] += 1
                ins.then_inc(dve_chain, 1)
                dve.wait_ge(dve_chain, chain[0])

            def arrived(g):
                dve.wait_ge(work_done, g.done)
                return work[:, g.bank, :]

            tt, ts, stt = nc.vector.tensor_tensor, nc.vector.tensor_scalar, nc.vector.scalar_tensor_tensor
            for t in range(IN_BANKS):
                bank = arrived(Group(("in", t)))
                nc.vector.tensor_copy(hT[:, 2 * t:2 * t + 2, :].rearrange("p t n -> p (t n)"), bank[:, :])\
                    .then_inc(h_ready, 1)

            def normalise(l, part):
                n = 2 * l + part
                dve.wait_ge(rstd_ready, n + 1)
                if n == 0:
                    dve.wait_ge(params_loaded, 16 * PARAMS)
                for k in range(KT):
                    stt(xnT[:, k, :], hT[:, k, :], gains[:, n, k:k + 1], rstd[:, :], ALU.mult, ALU.mult)\
                        .then_inc(xn_ready, 1)

            normalise(0, 0)

            dve.wait_ge(dt_ready, 1)
            link(ts(lr, lam[:, 0, :], -1e-4, None, ALU.min))
            link(tt(decay, lr, dt, ALU.mult))
            link(tt(angle, lam[:, 1, :], dt, ALU.mult))
            magic = 1.5 * 2.0 ** 23
            link(ts(turns, angle, 1.0 / (2 * math.pi), magic, ALU.mult, ALU.add))
            link(ts(turns, turns, -magic, None, ALU.add))
            two_pi = [6.28125, 0.0019350051879882812, 3.0199159819567633e-07]
            link(stt(reduced, turns, -two_pi[0], angle, ALU.mult, ALU.add))
            link(stt(reduced, turns, -two_pi[1], reduced, ALU.mult, ALU.add))
            link(stt(reduced, turns, -two_pi[2], reduced, ALU.mult, ALU.add))
            link(ts(reduced, reduced, 3.1415925, -3.1415925, ALU.min, ALU.max))
            link(ts(upright, reduced, -1.0, None, ALU.mult))
            link(tt(upright, reduced, upright, ALU.max))
            ts(upright, upright, -1.0, math.pi / 2, ALU.mult, ALU.add).then_inc(angle_ready, 1)
            li = lam[:, 1, :]
            link(tt(den, lr, lr, ALU.mult))
            link(tt(tmp1, li, li, ALU.mult))
            link(tt(den, den, tmp1, ALU.add))
            link(nc.vector.reciprocal(den, den))
            dve.wait_ge(sincos_ready, 3)
            link(tt(nr, mag, cos1, ALU.mult))
            link(ts(nr, nr, -1.0, None, ALU.add))
            link(tt(tmp2, mag, sin1, ALU.mult))
            link(tt(f_re, nr, lr, ALU.mult))
            link(tt(tmp1, tmp2, li, ALU.mult))
            link(tt(f_re, f_re, tmp1, ALU.add))
            link(tt(f_re, f_re, den, ALU.mult))
            link(tt(f_im, tmp2, lr, ALU.mult))
            link(tt(tmp1, nr, li, ALU.mult))
            link(tt(f_im, f_im, tmp1, ALU.subtract))
            tt(f_im, f_im, den, ALU.mult).then_inc(f_ready, 1)

            prod = vtmp[:, 0, :]
            for l in range(DEPTH):
                if l:
                    normalise(l, 0)
                for kind, t in STEPS:
                    if kind == "k":
                        bank = arrived(Group((l, kind, t)))
                        nc.vector.tensor_copy(kT[:, 2 * t:2 * t + 2, :].rearrange("p t n -> p (t n)"), bank[:, :])\
                            .then_inc(k_ready, 1)
                    elif kind == "v":
                        bank = arrived(Group((l, kind, t)))
                        nc.vector.tensor_copy(v[:, t, :], bank[:, :]).then_inc(v_ready, 1)
                    elif kind == "u":
                        bank = arrived(Group((l, kind, t)))
                        nc.vector.tensor_copy(uT[:, :, :].rearrange("p t n -> p (t n)"), bank[:, :])\
                            .then_inc(u_ready, 1)
                    elif kind == "softplus":
                        dve.wait_ge(log_ready, 2 * l + t + 1)
                        stt(attn[:, :, :], attn_z, 0.0, attn[:, :, :], ALU.max, ALU.add).then_inc(stay_ready, 1)
                    elif kind == "attend":
                        dve.wait_ge(attn_done, 2 * l + t + 1)
                        nc.vector.tensor_copy(qT[:, 2 * t:2 * t + 2, :], acc[:, 0:2, 0:L]).then_inc(attn_read, 1)
                    elif kind == "c":
                        bank = arrived(Group((l, kind, t)))
                        dve.wait_ge(h_conv_ready, l + 1)
                        tt(uconv[:, :, 2:L + 2], bank[:, :].rearrange("p (t n) -> p t n", n=L), hconv[:, :, :],
                           ALU.mult).then_inc(conv_u_ready, 1)
                        dve.wait_ge(conv_u_ready, l + 1)
                        dve.wait_ge(consts_made, 4)
                        for a in range(CT):
                            link(ts(hconv[:, a, :], uconv[:, a, 0:L], convw[:, l, 0, a:a + 1], None, ALU.mult))
                        for tap in (1, 2):
                            for a in range(CT):
                                link(stt(hconv[:, a, :], uconv[:, a, tap:tap + L], convw[:, l, tap, a:a + 1],
                                         hconv[:, a, :], ALU.mult, ALU.add))
                        dve.wait_ge(b_conv_ready, l + 1)
                        tt(hconv[:, :, :], hconv[:, :, :], bconv[:, :, :], ALU.mult).then_inc(conv_ready, 1)
                    elif kind == "bu":
                        n = l * SJ + t
                        bank = arrived(Group((l, kind, t)))
                        dve.wait_ge(tables_ready, l + 1)
                        if t >= 4:
                            dve.wait_ge(states_used, n - 3)
                        re, im = bank[:, 0:L], bank[:, L:2 * L]
                        s_re, s_im = sring[:, t % 4, 0, :], sring[:, t % 4, 1, :]
                        tt(s_re, re, cosT[:, t, :], ALU.mult)
                        tt(s_im, im, cosT[:, t, :], ALU.mult)
                        tt(vtmp[:, 0, :], im, sinT[:, t, :], ALU.mult)
                        tt(vtmp[:, 1, :], re, sinT[:, t, :], ALU.mult).then_inc(bu_read, 1)
                        dve.wait_ge(bu_read, n + 1)
                        link(tt(s_re, s_re, vtmp[:, 0, :], ALU.add))
                        link(tt(s_im, s_im, vtmp[:, 1, :], ALU.subtract))
                        step = mag[:, n:n + 1].to_broadcast([P, L])
                        for s in (s_re, s_im):
                            nc.vector.tensor_tensor_scan(s, step, s, 0.0, ALU.mult, ALU.add).then_inc(scanned, 1)
                    elif kind == "gelu":
                        dve.wait_ge(states_used, l * SJ + SJ)
                        for a in range(CT):
                            stt(uT[:, a, :], uT[:, a, :], dskip[:, l, a:a + 1], ssm_y[:, a, :], ALU.mult, ALU.add)\
                                .then_inc(gelu_in, 1)
                    elif kind == "glu":
                        dve.wait_ge(glu_ready, l + 1)
                        tt(uT[:, :, :], uT[:, :, :], bconv[:, :, :], ALU.mult).then_inc(yb_ready, 1)
                    elif kind in ("gA", "gB", "gC"):
                        n = gate_number(l, kind[1], t)
                        bank = arrived(Group((l, kind, t)))
                        dve.wait_ge(sig_ready, n + 1)
                        dst = merged[:, t, :] if kind == "gC" else prod
                        tt(dst, sig[:, n % 2, :], bank[:, L:2 * L], ALU.mult).then_inc(gate_used, 1)
                        if kind != "gC":
                            dve.wait_ge(gate_used, n + 1)
                            last = tt(merged[:, t, :], merged[:, t, :], prod, ALU.add)
                            if kind == "gA":
                                link(last)
                            else:
                                last.then_inc(merged_ready, 1)
                                dve.wait_ge(merged_ready, l * KT + t + 1)
                    elif kind == "wo":
                        bank = arrived(Group((l, kind, t)))
                        tt(hT[:, t, :], hT[:, t, :], bank[:, 0:L], ALU.add).then_inc(h_ready, 1)
                normalise(l, 1)
                if l == 0:
                    for n in range(FFN_TILES):
                        c = n // FT
                        bank = arrived(Group(("dense", n)))
                        dve.wait_ge(silu_ready, n + 1)
                        if c >= 2:
                            dve.wait_ge(down_chunk, c - 1)
                        tt(hid[:, c % 2, n % FT, :], sig[:, n % 2, :], bank[:, L:2 * L], ALU.mult)\
                            .then_inc(hid_ready, 1)
                    dve.wait_ge(down_chunk, NCH)
                    for b in range(4):
                        tt(hT[:, 2 * b:2 * b + 2, :].rearrange("p t n -> p (t n)"),
                           hT[:, 2 * b:2 * b + 2, :].rearrange("p t n -> p (t n)"), acc[:, b, :], ALU.add)\
                            .then_inc(h_ready, 1)

            bank = arrived(Group(("router", 0)))
            nc.vector.tensor_copy(logits[:, :, :].rearrange("p t n -> p (t n)"), bank[:, 0:TT * NE])\
                .then_inc(logits_ready, 1)
            dve.wait_ge(logits_ready, 1)
            for t in range(TT):
                link(nc.vector.max(stat[:, t, :], logits[:, t, :]))
                link(ts(order[:, t, :], slot_no[:, 0:NE], -1.0, float(NE), ALU.mult, ALU.add))
            for t in range(TT):
                link(stt(mask1[:, t, :], logits[:, t, :], stat[:, t, 0:1], order[:, t, :], ALU.is_equal, ALU.mult))
                link(nc.vector.reduce_max(stat[:, t, 7:8], mask1[:, t, :], AX.X))
                link(ts(mask1[:, t, :], mask1[:, t, :], stat[:, t, 7:8], None, ALU.is_equal))
                link(stt(mask2[:, t, :], logits[:, t, :], stat[:, t, 1:2], order[:, t, :], ALU.is_equal, ALU.mult))
                link(ts(chosen[:, t, :], mask1[:, t, :], -1.0, 1.0, ALU.mult, ALU.add))
                link(tt(mask2[:, t, :], mask2[:, t, :], chosen[:, t, :], ALU.mult))
                link(nc.vector.reduce_max(stat[:, t, 7:8], mask2[:, t, :], AX.X))
                link(ts(mask2[:, t, :], mask2[:, t, :], stat[:, t, 7:8], None, ALU.is_equal))
                link(tt(chosen[:, t, :], mask1[:, t, :], mask2[:, t, :], ALU.add))
            ts(rest[:, :, :], chosen[:, :, :], -1.0, None, ALU.mult).then_inc(chosen_ready, 1)
            tt(stat[:, :, 2:3], stat[:, :, 1:2], stat[:, :, 0:1], ALU.subtract).then_inc(diff_ready, 1)
            for t in range(2 * TT):
                bank = arrived(Group(("tok", 2 * TT + t)))
                nc.vector.tensor_copy(h_tok[:, t // 2, (t % 2) * 512:(t % 2) * 512 + 512], bank[:, :])\
                    .then_inc(h_tok_ready, 1)
            dve.wait_ge(expd_ready, 1)
            link(ts(stat[:, :, 4:5], stat[:, :, 3:4], 1.0, None, ALU.add))
            link(nc.vector.reciprocal(stat[:, :, 5:6], stat[:, :, 4:5]))
            link(tt(stat[:, :, 6:7], stat[:, :, 3:4], stat[:, :, 5:6], ALU.mult))
            for t in range(TT):
                link(ts(mask1[:, t, :], mask1[:, t, :], stat[:, t, 5:6], None, ALU.mult))
                for r in range(ROUNDS):
                    link(stt(wgt_c[:, t, r * NE:r * NE + NE], mask2[:, t, :], stat[:, t, 6:7], mask1[:, t, :],
                             ALU.mult, ALU.add))
            bank = arrived(Group(("rank", 0)))
            nc.vector.tensor_copy(neg_rank[:, :, :].rearrange("p t n -> p (t n)"), bank[:, 0:(TT + 1) * NE])\
                .then_inc(rank_read, 1)
            dve.wait_ge(rank_read, 1)
            link(stt(order[:, :, :], neg_rank[:, 0:TT, :], -1.0, rest[:, :, :], ALU.add, ALU.mult))
            for r in range(ROUNDS):
                link(ts(rank_c[:, :, r * NE:r * NE + NE], order[:, :, :], -1.0 - SLOTS * r, None, ALU.add))

            def build_pick(c):
                for t in range(TT):
                    ts(pick[:, t, :], slot_no[:, :], rank_c[:, t, c], None, ALU.is_equal)
                    last = ts(wpick[:, t, :], slot_no[:, :], rank_c[:, t, c], wgt_c[:, t, c], ALU.is_equal,
                              ALU.mult)
                last.then_inc(pick_ready, 1)

            build_pick(slice(0, 1))
            for r in range(1, ROUNDS):
                link(ts(active[:, (r - 1) * NE:r * NE], neg_rank[:, TT, :], float(-SLOTS * r), None, ALU.is_lt))
            link(nc.vector.tensor_tensor_scan(place, active, active, 0.0, ALU.add, ALU.max))
            link(tt(value, active, slot_no[:, NE:CAND], ALU.mult))
            link(tt(grid[:, :, :], place.unsqueeze(1).to_broadcast([P, XC, XC]),
                    slot_no[:, 1:XC + 1].unsqueeze(2).to_broadcast([P, XC, XC]), ALU.is_equal))
            link(tt(grid[:, :, :], grid[:, :, :], value.unsqueeze(1).to_broadcast([P, XC, XC]), ALU.mult))
            link(nc.vector.reduce_sum(listf[:, NE:CAND], grid[:, :, :], AX.X))
            link(nc.vector.tensor_copy(listf[:, 0:NE], slot_no[:, 0:NE]))
            link(ts(listf[:, CAND:CAND + 1], slot_no[:, 0:1], 0.0, None, ALU.mult))
            link(ts(listf[:, CAND + 1:CAND + 2], place[:, XC - 1:XC], float(NE), None, ALU.add))
            nc.vector.tensor_copy(items[:, :], listf).then_inc(items_ready, 1)
            dve.wait_ge(items_ready, 1)
            n_items = dve.value_load(items[0:1, CAND + 1:CAND + 2], min_val=NE, max_val=CAND)
            with dve.Fori(0, n_items) as i:
                for n in range(FFN_TILES):
                    c = n // FT
                    if n == FT:
                        dve.wait_ge(wpick_turned, i + 1)
                        cand = dve.value_load(items[0:1, bass.ds(i + 1, 1)], min_val=0, max_val=CAND - 1)
                        build_pick(bass.ds(cand, 1))
                    if n % FT == 0:
                        dve.wait_ge(down_chunk, i * NCH + (NCH + c - (c > 0)))
                    bank = work[:, Group(("f", n), i).bank, :]
                    dve.wait_ge(silu_ready, i * FFN_TILES + (FFN_TILES + n + 1))
                    tt(ehid[:, c % 2, n % FT, :], sig[:, n % 2, 0:SLOTS], bank[:, SLOTS:2 * SLOTS], ALU.mult)\
                        .then_inc(hid_ready, 1)
                dve.wait_ge(down_chunk, i * NCH + 2 * NCH)
                for b in range(2):
                    nc.vector.tensor_copy(yT[:, b * HALF:b * HALF + HALF, :].rearrange("p t n -> p (t n)"),
                                          acc[:, b, 0:HALF * SLOTS]).then_inc(yT_ready, 1)
                dve.wait_ge(h_tok_ready, i * 2 * TT + 2 * TT)
                for t in range(2 * TT):
                    bank = arrived(Group(("comb", t), i))
                    h = h_tok[:, t // 2, (t % 2) * 512:(t % 2) * 512 + 512]
                    tt(h, h, bank[:, :], ALU.add).then_inc(h_tok_ready, 1)
            dve.wait_ge(final_rstd, 1)
            dve.wait_ge(row_loaded, 16)
            for t in range(TT):
                stt(out_tile[:, t, :], h_tok[:, t, :], sumsq[:, t:t + 1], g_row, ALU.mult, ALU.mult)\
                    .then_inc(rows_ready, 1)

        @block.gpsimd
        def _(pool):
            chain = [0]

            def link(ins):
                chain[0] += 1
                ins.then_inc(pool_chain, 1)
                pool.wait_ge(pool_chain, chain[0])

            tt, ts = nc.gpsimd.tensor_tensor, nc.gpsimd.tensor_scalar
            link(nc.gpsimd.memset(ident[:, :], 0.0))
            nc.gpsimd.affine_select(out=ident[:, :], in_=ident[:, :], compare_op=ALU.not_equal, fill=1.0, base=0,
                                    pattern=[[-1, P]], channel_multiplier=1).then_inc(consts_made, 1)
            link(nc.gpsimd.memset(neg_incl[:, :], -1.0))
            nc.gpsimd.affine_select(out=neg_incl[:, :], in_=neg_incl[:, :], compare_op=ALU.is_ge, fill=0.0,
                                    base=0, pattern=[[-1, P]], channel_multiplier=1).then_inc(consts_made, 1)
            link(nc.gpsimd.memset(bias[:, 0:1], EPS))
            link(nc.gpsimd.memset(bias[:, 1:2], 1.0))
            link(nc.gpsimd.memset(uconv[:, :, 0:2], 0.0))
            nc.gpsimd.memset(neg_ones[:, :], -1.0).then_inc(consts_made, 1)
            numbers = vtmp[:, 0, 0:SLOTS].bitcast(I32)
            link(nc.gpsimd.iota(numbers, pattern=[[1, SLOTS]], base=0, channel_multiplier=0))
            nc.gpsimd.tensor_copy(slot_no[:, :], numbers).then_inc(consts_made, 1)

            def ssm_parameters(l):
                if l:
                    pool.wait_ge(states_used, l * SJ)
                    pool.wait_ge(work_done, Group((l - 1, "glu", 0)).done)
                js = slice(l * SJ, l * SJ + SJ)
                for c, (b_src, c_src) in enumerate(((b_re, c_re), (b_im, c_im))):
                    pool.dma_start(braw[:, c, :, :], b_src[l].rearrange("g p h -> (g p) h")
                                   .rearrange("(j s) h -> s j h", s=P)).then_inc(ssm_loaded, 16)
                    pool.dma_start(craw[:, c, :, :], c_src[l].rearrange("g p h -> (g p) h")
                                   .rearrange("(j s) h -> s j h", s=P)).then_inc(ssm_loaded, 16)
                pool.dma_start(wglu[:, :, :], rows(w_glu[l])).then_inc(glu_loaded, 16)
                link(nc.gpsimd.memset(bbp[:, :, :], 0.0))
                link(nc.gpsimd.memset(cblk[:, :, :, :], 0.0))
                pool.wait_ge(ssm_loaded, 64 * (l + 1))
                pool.wait_ge(f_ready, 1)
                fr = f_re[:, js].unsqueeze(2).to_broadcast([P, SJ, GH])
                fi = f_im[:, js].unsqueeze(2).to_broadcast([P, SJ, GH])
                m = [rtmp[:, q, 0:SJ * GH].rearrange("p (j h) -> p j h", h=GH) for q in range(4)]
                link(tt(m[0], braw[:, 0, :, :], fr, ALU.mult))
                link(tt(m[1], braw[:, 1, :, :], fi, ALU.mult))
                link(tt(m[2], braw[:, 1, :, :], fr, ALU.mult))
                link(tt(m[3], braw[:, 0, :, :], fi, ALU.mult))
                for par in range(2):
                    r = slice(par * P // 2, par * P // 2 + P // 2)
                    hs = slice(par * GH, par * GH + GH)
                    for c, op in ((0, ALU.subtract), (1, ALU.add)):
                        dst = bbp[r, c, :].rearrange("p (j h) -> p j h", h=2 * GH)[:, :, hs]
                        link(tt(dst, m[2 * c][r], m[2 * c + 1][r], op))
                    link(ts(cblk[r, 0, :, hs], craw[r, 0, :, :], 1.0, None, ALU.mult))
                    link(ts(cblk[r, 1, :, hs], craw[r, 1, :, :], -1.0, None, ALU.mult))
                nc.gpsimd.memset(cosT[:, :, 0:1], 1.0).then_inc(bbp_ready, 1)
                pc, ps, p2, p3, p4 = [power[:, q, :] for q in range(5)]
                link(nc.gpsimd.memset(sinT[:, :, 0:1], 0.0))
                link(nc.gpsimd.tensor_copy(pc, cos1[:, js]))
                nc.gpsimd.tensor_copy(ps, sin1[:, js]).then_inc(c_ready, 1)
                pool.wait_ge(c_ready, l + 1)
                pool.wait_ge(bbp_ready, l + 1)
                n = 1
                while n < L:
                    old, new = slice(0, n), slice(n, 2 * n)
                    bc = pc.unsqueeze(2).to_broadcast([P, SJ, n])
                    bs = ps.unsqueeze(2).to_broadcast([P, SJ, n])
                    tmp = rtmp[:, :, :].rearrange("p t n -> p (t n)")[:, 0:SJ * n].rearrange("p (j n) -> p j n", n=n)
                    tt(cosT[:, :, new], cosT[:, :, old], bc, ALU.mult)
                    link(tt(tmp, sinT[:, :, old], bs, ALU.mult))
                    tt(sinT[:, :, new], sinT[:, :, old], bc, ALU.mult)
                    link(tt(cosT[:, :, new], cosT[:, :, new], tmp, ALU.subtract))
                    link(tt(tmp, cosT[:, :, old], bs, ALU.mult))
                    last = tt(sinT[:, :, new], sinT[:, :, new], tmp, ALU.add)
                    n *= 2
                    if n == L:
                        last.then_inc(tables_ready, 1)
                        break
                    link(last)
                    link(tt(p2, pc, pc, ALU.mult))
                    link(tt(p3, ps, ps, ALU.mult))
                    link(tt(p4, pc, ps, ALU.mult))
                    link(tt(pc, p2, p3, ALU.subtract))
                    link(tt(ps, p4, p4, ALU.add))

            for l in range(DEPTH):
                ssm_parameters(l)
                for kind, t in STEPS:
                    if kind == "softplus":
                        pool.wait_ge(stay_ready, 2 * l + t + 1)
                        for lo in (0, L):
                            blk = attn[:, :, lo:lo + P]
                            last = nc.gpsimd.affine_select(out=blk, in_=blk, compare_op=ALU.is_gt, fill=0.0,
                                                           base=0, pattern=[[0, HB], [1, P]],
                                                           channel_multiplier=-1)
                            if lo == 0:
                                link(last)
                        last.then_inc(stay_masked, 1)
                    elif kind == "tail":
                        pool.wait_ge(w_ready, 2 * l + t + 1)
                        for lo in (0, L):
                            blk = attn[:, :, lo:lo + P]
                            last = nc.gpsimd.affine_select(out=blk, in_=blk, compare_op=ALU.is_gt, fill=0.0,
                                                           base=0, pattern=[[0, HB], [1, P]],
                                                           channel_multiplier=-1)
                            if lo == 0:
                                link(last)
                        last.then_inc(w_masked, 1)
                    elif kind == "bu":
                        pool.wait_ge(scanned, 2 * (l * SJ + t + 1))
                        s_re, s_im = sring[:, t % 4, 0, :], sring[:, t % 4, 1, :]
                        tt(rtmp[:, 0, :], s_re, cosT[:, t, :], ALU.mult)
                        tt(rtmp[:, 1, :], s_im, sinT[:, t, :], ALU.mult)
                        tt(rtmp[:, 2, :], s_re, sinT[:, t, :], ALU.mult)
                        link(tt(rtmp[:, 3, :], s_im, cosT[:, t, :], ALU.mult))
                        link(tt(s_re, rtmp[:, 0, :], rtmp[:, 1, :], ALU.subtract))
                        tt(s_im, rtmp[:, 2, :], rtmp[:, 3, :], ALU.add).then_inc(states_ready, 1)
                        pool.wait_ge(states_ready, l * SJ + t + 1)


_NAMES = ["x", "norm_mix", "w_in", "ssm_lambda_re", "ssm_lambda_im", "ssm_log_dt", "ssm_b_re", "ssm_b_im",
          "ssm_c_re", "ssm_c_im", "ssm_d", "ssm_w_glu", "conv_w", "w_br_a", "w_br_b", "w_br_c", "w_out",
          "norm_ffn", "dense_w_gate", "dense_w_up", "dense_w_down", "moe_w_router", "moe_w_gate", "moe_w_up",
          "moe_w_down", "final_norm"]


def _lay_out(inputs):
    import numpy as np

    a = {n: np.asarray(inputs[n]) for n in _NAMES}
    depth, d = a["norm_mix"].shape
    p = 128
    a["x"] = a["x"][0]
    for n in ("norm_mix", "norm_ffn"):
        a[n] = a[n].reshape(depth, d // p, p).transpose(0, 2, 1)
    for n in ("ssm_lambda_re", "ssm_lambda_im"):
        a[n] = a[n].reshape(depth, -1, p).transpose(2, 0, 1)
    a["ssm_log_dt"] = a["ssm_log_dt"].reshape(depth, -1, 2).transpose(2, 0, 1)
    for n in ("ssm_c_re", "ssm_c_im"):
        a[n] = a[n].transpose(0, 1, 3, 2)
    a["ssm_d"] = a["ssm_d"].reshape(depth, -1, p).transpose(2, 0, 1)
    a["conv_w"] = a["conv_w"].reshape(depth, a["conv_w"].shape[1], -1, p).transpose(3, 0, 1, 2)
    a["final_norm"] = a["final_norm"].reshape(1, d)
    return {n: np.ascontiguousarray(v) for n, v in a.items()}


def kernel(**inputs):
    import numpy as _np
    import concourse.bacc as _bacc
    from concourse import mybir as _mybir
    from concourse.bass_utils import run_bass_kernel_spmd as _run

    nc = _bacc.Bacc("TRN2", target_bir_lowering=False, num_devices=1)
    arrays, args = {}, []
    for name, a in _lay_out(inputs).items():
        arrays[f"in_{name}"] = a
        args.append(nc.dram_tensor(f"in_{name}", a.shape, _mybir.dt.from_np(a.dtype), kind="ExternalInput").ap())
    shape = arrays["in_x"].shape
    out = nc.dram_tensor("out", shape, _mybir.dt.from_np(_np.dtype("float32")), kind="ExternalOutput").ap()
    trunk_kernel(nc, *args, out)
    r = _run(nc, [arrays], core_ids=[0])
    return r.results[0]["out"].reshape(1, *shape)
```

```python
import math

import concourse.bass as bass
from concourse import mybir
from contextlib import ExitStack


def trunk_kernel(nc, x, gain_mix, w_in, lam_re, lam_im, log_dt, b_re, b_im, c_re, c_im, ssm_d, w_glu,
                 conv_w, w_br_a, w_br_b, w_br_c, w_out, gain_ffn, dense_gate, dense_up, dense_down,
                 w_router, moe_gate, moe_up, moe_down, gain_final, out):
    F32 = mybir.dt.float32
    F32R = mybir.dt.float32r
    I32 = mybir.dt.int32
    ALU = mybir.AluOpType
    ACT = mybir.ActivationFunctionType
    AX = mybir.AxisListType

    P = 128
    L = x.shape[0]
    D = x.shape[1]
    DEPTH = w_in.shape[0]
    KT = D // P
    TT = L // P
    UC = 256
    UW = UC * KT
    CW2 = 512
    DH = 64
    QW = w_br_a.shape[1]
    HEADS = QW // DH
    HB = 4
    NB = HEADS // HB
    CW = w_br_b.shape[1]
    CT = CW // P
    GH = b_re.shape[3]
    SJ = b_re.shape[1] * b_re.shape[2] // P
    FF = dense_gate.shape[2]
    NHC = FF // UC
    FT = UC // P
    NCH = FF // CW2
    HT = CW2 // P
    NE = w_router.shape[2]
    SLOTS = 96
    ROUNDS = -(-L // SLOTS)
    CAND = ROUNDS * NE
    EPS = 1e-6
    SCALE = DH ** -0.5
    GATE0 = 3 * QW + 4 * CW

    def cols(w, c):
        return w[:, c:c + UC].rearrange("(k p) n -> p k n", p=P)

    def rows(w):
        return w.rearrange("(k p) n -> p k n", p=P)

    GU = D // UC
    MIXER = (["q0", "q1", "k0", "k1", "v0", "v1", "u0", "h0", "b0", "c0"] + [f"gC{n}" for n in range(GU)]
             + ["gA0"] + [f"brA{n}" for n in range(QW // UC)] + [f"gA{n}" for n in range(1, GU)]
             + [f"gB{n}" for n in range(GU)] + [f"wo{n}" for n in range(GU)])
    DENSE = []
    for c in range(NHC):
        DENSE += [f"G{c}", f"U{c}"] + ([f"D{c - 1}"] if c else [])
    DENSE += [f"D{NHC - 1}"]
    EXPERT = []
    for c in range(NCH):
        EXPERT += [f"G{2 * c}", f"G{2 * c + 1}", f"U{2 * c}", f"U{2 * c + 1}"]
        EXPERT += [f"D{2 * c - 2}", f"D{2 * c - 1}"] if c else []
    EXPERT += [f"D{NHC - 2}", f"D{NHC - 1}"]
    IU = len(EXPERT)
    RING = 7
    PARTS = 3
    STREAM = [(0, n) for n in MIXER + DENSE] + [(1, n) for n in MIXER]
    SPLIT = [u for u in STREAM if not u[1].startswith("br")]
    assert IU % RING == 0 and IU % PARTS == 0 and STREAM[-RING:] == SPLIT[-RING:] and CW == UC
    S0 = len(SPLIT)
    AHEAD = 3

    GATE_OF = {"A": 0, "B": 1, "C": 2}

    def mixer_source(l, name):
        n = int(name[-1])
        if name[:-1] in ("q", "k", "v"):
            return cols(w_in[l], QW * "qkv".index(name[0]) + UC * n)
        if name[:-1] in ("u", "h", "b", "c"):
            return cols(w_in[l], 3 * QW + CW * "uhbc".index(name[0]))
        if name[0] == "g":
            return cols(w_in[l], GATE0 + GATE_OF[name[1]] * D + UC * n)
        if name[:2] == "br":
            w = {"A": w_br_a, "B": w_br_b, "C": w_br_c}[name[2]]
            return rows(w[l, UC * n:UC * n + UC, :])
        return cols(w_out[l], UC * n)

    def unit_of(kind, t):
        if kind in ("q", "k", "v", "u", "h", "b", "c"):
            return f"{kind}{t}"
        if kind in ("gA", "gB", "gC", "wo") and t % 2 == 0:
            return f"{kind}{t // 2}"
        return None

    STEPS = [("q", 0), ("q", 1), ("k", 0), ("k", 1), ("v", 0), ("v", 1), ("z", 0), ("bbT", 0),
             ("u", 0), ("softplus", 0), ("h", 0), ("b", 0), ("c", 0), ("tail", 0)]
    BU_AFTER = [0, 1, 3, 4, 6, 7, 9, 10]
    YS_AFTER = [3, 4, 6, 7, 9, 10, 12, 13]
    for t in range(2 * KT):
        STEPS.append(("gC", t) if t < KT else ("gA", t - KT))
        if t == 1:
            STEPS.append(("attend", 0))
        if t == 2:
            STEPS.append(("z", 1))
        if t == 3:
            STEPS.append(("softplus", 1))
        if t == 4:
            STEPS.append(("tail", 1))
        if t == KT - 1:
            STEPS.append(("attend", 1))
        if t in YS_AFTER:
            STEPS.append(("ys", YS_AFTER.index(t)))
        if t in BU_AFTER:
            STEPS.append(("bu", BU_AFTER.index(t)))
        if t == 14:
            STEPS.append(("gelu", 0))
    STEPS.append(("glu", 0))
    STEPS += [("gB", t) for t in range(KT)]
    STEPS += [("wo", t) for t in range(KT)]

    GROUPS = [("in", t) for t in range(KT * TT // 4)]
    NOT_WORK = ("z", "softplus", "tail", "attend", "ys", "gelu")
    for l in range(DEPTH):
        GROUPS.append(("rms", l, 0))
        GROUPS += [(l, *s) for s in STEPS if s[0] not in NOT_WORK]
        GROUPS.append(("rms", l, 1))
        if l == 0:
            GROUPS += [("dense", t) for t in range(NHC * FT)]
    GROUPS += [("router", 0)] + [("tok", t) for t in range(4 * TT)] + [("rank", 0)]
    GROUPS += [("gather0", 0), ("gather0", 1)]
    ITEM0 = len(GROUPS)
    ITEM_GROUPS = []
    for c in range(NCH):
        ITEM_GROUPS += [("g", c)] + ([("t", c - 1)] if c else []) + [("u", c)]
    ITEM_GROUPS += [("gather", 0), ("t", NCH - 1), ("gather", 1)] + [("comb", t) for t in range(2 * TT)]
    WB = 3
    assert len(ITEM_GROUPS) % WB == 0
    IG = len(ITEM_GROUPS)
    INDEX = {g: n for n, g in enumerate(GROUPS)}
    ITEM_INDEX = {g: n for n, g in enumerate(ITEM_GROUPS)}

    class Group:

        def __init__(self, key, item=None):
            n = INDEX[key] if item is None else ITEM0 + ITEM_INDEX[key]
            self.n = n
            self.bank = n % WB
            self.done = n + 1 if item is None else item * IG + (n + 1)

    ctx = ExitStack()
    with ctx:
        def sb(name, shape, dt=F32):
            return ctx.enter_context(nc.sbuf_tensor(name, shape, dt))

        def sem(name):
            return ctx.enter_context(nc.semaphore(name))

        ring = sb("ring", [P, RING, UW])
        br_slot = sb("br_slot", [P, UW])
        parts = sb("parts", [P, PARTS, 2, UW], F32R)
        xs = sb("xs", [P, 2 * KT * L], F32R)
        hs = sb("hs", [P, 4 * FT * L], F32R)
        hT = sb("hT", [P, KT, L])
        ident = sb("ident", [P, P])
        neg_incl = sb("neg_incl", [P, P])
        neg_ones = sb("neg_ones", [P, P])
        rstd = sb("rstd", [P, L])
        gains = sb("gains", [P, 2 * DEPTH, KT])
        lam = sb("lam", [P, 2, DEPTH * SJ])
        logdt = sb("logdt", [P, DEPTH * SJ])
        bias = sb("bias", [P, 2])
        slot_no = sb("slot_no", [P, SLOTS])
        dskip = sb("dskip", [P, DEPTH, CT])
        convw = sb("convw", [P, DEPTH, 3, CT])
        small = sb("small", [P, 16, DEPTH * SJ])
        (dt, lr, decay, angle, mag, turns, reduced, upright, sin1, cos1, den, tmp1, nr, tmp2, f_re,
         f_im) = [small[:, n, :] for n in range(16)]
        power = sb("power", [P, 5, SJ])
        wr = sb("wr", [P, KT, NE])
        wglu = sb("wglu", [P, CT, CW])
        cblk = sb("cblk", [P, 2, SJ, 2 * GH])
        bbT = sb("bbT", [P, 4, P])
        sig = sb("sig", [P, 2, L])
        ARENA = 16392
        arena = sb("arena", [P, ARENA])
        at = [0]

        def carve(n):
            at[0] += n
            assert at[0] <= ARENA, at[0]
            return arena[:, at[0] - n:at[0]]

        qT = carve(QW // P * L).rearrange("p (t n) -> p t n", n=L)
        kT = carve(QW // P * L).rearrange("p (t n) -> p t n", n=L)
        v = carve(TT * QW).rearrange("p (t n) -> p t n", n=QW)
        AW = L + P
        attn = carve(HB * AW).rearrange("p (h n) -> p h n", n=AW)
        uT = carve(CT * L).rearrange("p (t n) -> p t n", n=L)
        hconv = carve(CT * L).rearrange("p (t n) -> p t n", n=L)
        bconv = carve(CT * L).rearrange("p (t n) -> p t n", n=L)
        uconv = carve(CT * (L + 2)).rearrange("p (t n) -> p t n", n=L + 2)
        cosT = carve(SJ * L).rearrange("p (j n) -> p j n", n=L)
        sinT = carve(SJ * L).rearrange("p (j n) -> p j n", n=L)
        vtmp = carve(2 * L).rearrange("p (t n) -> p t n", n=L)
        rtmp = carve(4 * L).rearrange("p (t n) -> p t n", n=L)
        sring = carve(4 * 2 * L).rearrange("p (t c n) -> p t c n", c=2, n=L)
        bbp = sring[:, 3, :, :]
        braw = sring[:, 2, 0, 0:2 * SJ * GH].rearrange("p (c j h) -> p c j h", c=2, h=GH)
        craw = sring[:, 2, 1, 0:2 * SJ * GH].rearrange("p (c j h) -> p c j h", c=2, h=GH)
        MERGED_AT = at[0]
        merged = carve(KT * L).rearrange("p (t n) -> p t n", n=L)
        xnT = merged
        x_in = arena[:, 0:TT * D].rearrange("p (t n) -> p t n", n=D)
        at[0] = 0
        hid = carve(2 * L).rearrange("p (b n) -> p b n", b=2)
        x_parts = [xs[:, q * KT * L:(q + 1) * KT * L].rearrange("p (k n) -> p k n", n=L) for q in range(2)]
        xe_parts = [xs[:, q * KT * SLOTS:(q + 1) * KT * SLOTS].rearrange("p (k n) -> p k n", n=SLOTS)
                    for q in range(2)]
        h_parts = hs[:, :].rearrange("p (b q f n) -> p b q f n", b=2, q=2, n=L)
        eh_parts = [hs[:, q * HT * SLOTS:(q + 1) * HT * SLOTS].rearrange("p (f n) -> p f n", n=SLOTS)
                    for q in range(2)]
        at[0] = 0
        esilu = carve(CW2)
        erow = carve(CW2)
        h_tok = carve(TT * D).rearrange("p (t n) -> p t n", n=D)
        xn_tok = carve(TT * D).rearrange("p (t n) -> p t n", n=D)
        y_tok = carve(D)
        pick = carve(TT * SLOTS).rearrange("p (t n) -> p t n", n=SLOTS)
        wpick = carve(TT * SLOTS).rearrange("p (t n) -> p t n", n=SLOTS)
        combine = carve(L)
        g_row = carve(D)
        rank_c = carve(TT * CAND).rearrange("p (t n) -> p t n", n=CAND)
        wgt_c = carve(TT * CAND).rearrange("p (t n) -> p t n", n=CAND)
        logits = carve(TT * NE).rearrange("p (t n) -> p t n", n=NE)
        mask1 = carve(TT * NE).rearrange("p (t n) -> p t n", n=NE)
        mask2 = carve(TT * NE).rearrange("p (t n) -> p t n", n=NE)
        chosen = carve(TT * NE).rearrange("p (t n) -> p t n", n=NE)
        rest = carve(TT * NE).rearrange("p (t n) -> p t n", n=NE)
        order = carve(TT * NE).rearrange("p (t n) -> p t n", n=NE)
        stat = carve(TT * 8).rearrange("p (t n) -> p t n", n=8)
        XC = CAND - NE
        active = carve(XC)
        place = carve(XC)
        value = carve(XC)
        grid = carve(XC * XC).rearrange("p (i c) -> p i c", c=XC)
        counts = carve(NE)
        listf = carve(CAND + 2)
        neg_rank = carve((TT + 1) * NE).rearrange("p (t n) -> p t n", n=NE)
        sumsq = carve(TT)
        assert at[0] <= MERGED_AT
        out_tile = xn_tok
        items = sb("items", [P, CAND + 2], I32)

        acc = ctx.enter_context(nc.psum_tensor("acc", [P, 4, 512], F32))
        ssm_y = ctx.enter_context(nc.psum_tensor("ssm_y", [P, CT, L], F32))
        work = ctx.enter_context(nc.psum_tensor("work", [P, WB, 512], F32))
        attn_z = acc[:, :, 0:AW]

        slot_full = [sem(f"slot_full{n}") for n in range(RING)]
        work_done = sem("work_done")
        x_loaded = [sem(f"x_loaded{half}") for half in range(2)]
        params_loaded = sem("params_loaded")
        ssm_loaded = sem("ssm_loaded")
        glu_loaded = sem("glu_loaded")
        wr_loaded = sem("wr_loaded")
        row_loaded = sem("row_loaded")
        consts_made = sem("consts_made")
        h_ready = sem("h_ready")
        sum_ready = sem("sum_ready")
        sq_ready = sem("sq_ready")
        rstd_ready = sem("rstd_ready")
        xn_ready = sem("xn_ready")
        q_ready = sem("q_ready")
        k_ready = sem("k_ready")
        v_ready = sem("v_ready")
        z_done = sem("z_done")
        log_ready = sem("log_ready")
        stay_ready = sem("stay_ready")
        stay_masked = sem("stay_masked")
        tail_done = sem("tail_done")
        w_ready = sem("w_ready")
        w_masked = sem("w_masked")
        attn_done = sem("attn_done")
        attn_read = sem("attn_read")
        h_conv_ready = sem("h_conv_ready")
        b_conv_ready = sem("b_conv_ready")
        conv_ready = sem("conv_ready")
        u_ready = sem("u_ready")
        dt_ready = sem("dt_ready")
        angle_ready = sem("angle_ready")
        sincos_ready = sem("sincos_ready")
        f_ready = sem("f_ready")
        bbp_ready = sem("bbp_ready")
        bbT_ready = sem("bbT_ready")
        c_ready = sem("c_ready")
        tables_ready = sem("tables_ready")
        scanned = sem("scanned")
        states_ready = sem("states_ready")
        states_used = sem("states_used")
        gelu_in = sem("gelu_in")
        gelu_out = sem("gelu_out")
        glu_ready = sem("glu_ready")
        yb_ready = sem("yb_ready")
        sig_ready = sem("sig_ready")
        merged_ready = sem("merged_ready")
        silu_ready = sem("silu_ready")
        hid_ready = sem("hid_ready")
        hi_ready = sem("hi_ready")
        lo_ready = sem("lo_ready")
        half_done = sem("half_done")
        br_full = sem("br_full")
        down_done = sem("down_done")
        xs_hi_ready = sem("xs_hi_ready")
        xs_ready = sem("xs_ready")
        hid_hi_ready = sem("hid_hi_ready")
        hid_split = sem("hid_split")
        esilu_ready = sem("esilu_ready")
        erow_ready = sem("erow_ready")
        eh_hi_ready = sem("eh_hi_ready")
        eh_ready = sem("eh_ready")
        xe_hi_ready = sem("xe_hi_ready")
        logits_ready = sem("logits_ready")
        chosen_ready = sem("chosen_ready")
        tok_ready = sem("tok_ready")
        items_ready = sem("items_ready")
        pick_ready = sem("pick_ready")
        wpick_ready = sem("wpick_ready")
        wpick_turned = sem("wpick_turned")
        combine_ready = sem("combine_ready")
        xe_ready = sem("xe_ready")
        y_ready = sem("y_ready")
        rms_read = sem("rms_read")
        conv_u_ready = sem("conv_u_ready")
        bu_read = sem("bu_read")
        gate_used = sem("gate_used")
        rank_read = sem("rank_read")
        diff_ready = sem("diff_ready")
        expd_ready = sem("expd_ready")
        h_tok_ready = sem("h_tok_ready")
        final_rstd = sem("final_rstd")
        rows_ready = sem("rows_ready")
        out_stored = sem("out_stored")
        act_chain = sem("act_chain")
        dve_chain = sem("dve_chain")
        pool_chain = sem("pool_chain")

        block = ctx.enter_context(nc.Block())
        DENSE_TILES = NHC * FT
        IN_BANKS = KT * TT // 4
        H_MIXED = [IN_BANKS, IN_BANKS + KT + 4]
        GATES = ["C", "A", "B"]

        def gate_number(l, branch, t):
            return (l * len(GATES) + GATES.index(branch)) * KT + t

        def reader(key, item=None):
            kind = key[0]
            if item is not None:
                t = key[1]
                return {"g": (esilu_ready, item * NCH + (t + 1)),
                        "u": (erow_ready, item * NCH + (t + 1)),
                        "t": (eh_ready, item * NCH + (t + 1)),
                        "gather": (xe_ready, item * 2 + (3 + t)),
                        "comb": (h_tok_ready, item * 2 * TT + (2 * TT + t + 1))}[kind]
            if kind == "in":
                return h_ready, key[1] + 1
            if kind == "rms":
                return rms_read, 2 * key[1] + key[2] + 1
            if kind == "dense":
                return hid_ready, key[1] + 1
            if kind == "router":
                return logits_ready, 1
            if kind == "tok":
                return (tok_ready, key[1] + 1) if key[1] < 2 * TT else (h_tok_ready, key[1] - 2 * TT + 1)
            if kind == "rank":
                return rank_read, 1
            if kind == "gather0":
                return xe_ready, key[1] + 1
            l, kind, t = key
            if kind[0] == "g" and kind[1:] in GATES:
                return gate_used, gate_number(l, kind[1], t) + 1
            return {"q": (q_ready, 2 * l + t + 1), "k": (k_ready, 2 * l + t + 1), "v": (v_ready, 2 * l + t + 1),
                    "bbT": (bbT_ready, l + 1), "u": (u_ready, l + 1), "h": (h_conv_ready, l + 1),
                    "b": (b_conv_ready, l + 1), "c": (conv_u_ready, l + 1), "bu": (bu_read, l * SJ + t + 1),
                    "glu": (glu_ready, l + 1), "wo": (h_ready, H_MIXED[l] + t + 1)}[kind]

        PARAMS = 2 + 2 + 2 * DEPTH + 2
        HALF = KT // 2

        def unit_view(flat, name, expert=False):
            n = D if name[0] == "D" or name[:2] == "br" else CW2 if expert else UC
            return flat.rearrange("p (k n) -> p k n", n=n)

        def used_up(l, name):
            n = int(name[-1]) if name[0] not in "GUD" else int(name[1:])
            if name[0] == "D":
                return down_done, n + 1
            if name[0] == "G":
                return half_done, n + 1
            if name[0] == "U":
                return work_done, Group(("dense", n * FT + FT - 1)).done
            if name[:2] in ("gA", "gB", "gC", "wo"):
                return work_done, Group((l, name[:2], 2 * n + 1)).done
            return work_done, Group((l, name[0], n)).done

        def item_used_up(name, i):
            n = int(name[1:])
            if name[0] == "D":
                return down_done, i * NHC + (NHC + n + 1)
            if n % 2 == 0:
                return half_done, i * NHC + (NHC + n + (name[0] == "U") + 1)
            return work_done, Group((name[0].lower(), n // 2), i).done

        def raw_unit(j):
            return ring[:, (len(STREAM) + j) % RING, :]

        class Splitter:

            def __init__(self, split):
                self.split, self.next = split, 0

            def upto(self, l, name):
                while self.next < min(SPLIT.index((l, name)) + AHEAD, S0):
                    self.split(self.next)
                    self.next += 1

            def upto_first(self, n):
                while self.next < n:
                    self.split(self.next)
                    self.next += 1

        FIRST = AHEAD - 1

        class ItemSplitter(Splitter):

            def __init__(self, split):
                self.split, self.next = split, FIRST

            def upto(self, name):
                self.upto_first(min(EXPERT.index(name) + AHEAD, IU))

        @block.sync
        def _(sp):
            for half in range(2):
                dh = slice(half * D // 2, (half + 1) * D // 2)
                sp.dma_start(x_in[:, :, dh], x[:, dh].rearrange("(t p) d -> p t d", p=P))\
                    .then_inc(x_loaded[half], 16)

            for n, (l, name) in enumerate(STREAM):
                if n == 1:
                    sp.wait_ge(params_loaded, 16 * PARAMS)
                if name in ("gC0", "gB0"):
                    if name == "gB0":
                        sp.wait_ge(work_done, Group((l, "gC", KT - 1)).done)
                    elif l:
                        sp.wait_ge(work_done, Group((l - 1, "gB", KT - 1)).done)
                    w = w_br_c[l] if name == "gC0" else w_br_b[l]
                    sp.dma_start(unit_view(br_slot[:, :], "br"), rows(w)).then_inc(br_full, 16)
                if n >= RING:
                    old_l, old = STREAM[n - RING]
                    if old[:2] == "br":
                        sp.wait_ge(work_done, Group((old_l, "g" + old[2], KT - 1)).done)
                    else:
                        sp.wait_ge(lo_ready, SPLIT.index((old_l, old)) + 1)
                if name[0] in "GUD":
                    c = int(name[1:])
                    src = {"G": dense_gate, "U": dense_up, "D": dense_down}[name[0]][0]
                    src = rows(src[UC * c:UC * c + UC, :]) if name[0] == "D" else cols(src, UC * c)
                else:
                    src = mixer_source(l, name)
                sp.dma_start(unit_view(ring[:, n % RING, :], name), src).then_inc(slot_full[n % RING], 16)

            def expert(i, e, units=IU):
                for j, name in enumerate(EXPERT[:units]):
                    n = int(name[1:])
                    src = {"G": moe_gate, "U": moe_up, "D": moe_down}[name[0]]
                    w = src[0, bass.ds(e, 1), :, :].rearrange("a k n -> (a k) n")
                    if name[0] == "D":
                        w = w[UC * n:UC * n + UC, :]
                    else:
                        w = w[(n % 2) * (D // 2):(n % 2 + 1) * (D // 2), (n // 2) * CW2:(n // 2 + 1) * CW2]
                    sp.wait_ge(lo_ready, i * IU + (S0 + j - RING + 1))
                    sp.dma_start(unit_view(raw_unit(j), name, True), rows(w))\
                        .then_inc(slot_full[(len(STREAM) + j) % RING], 16)

            with sp.Fori(0, NE) as i:
                expert(i, i)
            sp.wait_ge(items_ready, 1)
            n_items = sp.value_load(items[0:1, CAND + 1:CAND + 2], min_val=NE, max_val=CAND)
            with sp.If(n_items > NE):
                with sp.Fori(NE, n_items) as i:
                    c = sp.value_load(items[0:1, bass.ds(i, 1)], min_val=0, max_val=CAND - 1)
                    expert(i, c % NE)
            expert(n_items, 0, FIRST)
            for t in range(TT):
                sp.wait_ge(rows_ready, t + 1)
                sp.dma_start(out[t * P:t * P + P, :], out_tile[:, t, :]).then_inc(out_stored, 16)
            sp.wait_ge(out_stored, 16 * TT)

        @block.tensor
        def _(pe):
            def begin(g, item=None):
                n = g.n - WB
                if item is None:
                    if n >= 0:
                        pe.wait_ge(*reader(GROUPS[n]))
                elif n >= ITEM0:
                    pe.wait_ge(*reader(ITEM_GROUPS[n - ITEM0], item))
                else:
                    t = ITEM_GROUPS[n - ITEM0 + IG][1]
                    pe.wait_ge(h_tok_ready, item * 2 * TT + (t + 1))
                return work[:, g.bank, :]

            def weights(l, name):
                s = SPLIT.index((l, name))
                pe.wait_ge(lo_ready, s + 1)
                return [unit_view(parts[:, s % PARTS, q, :], name) for q in range(2)]

            def item_weights(name, i):
                j = EXPERT.index(name)
                pe.wait_ge(lo_ready, i * IU + (S0 + j + 1))
                return [unit_view(parts[:, (S0 + j) % PARTS, q, :], name, True) for q in range(2)]

            def raw_weights(l, name):
                n = STREAM.index((l, name))
                pe.wait_ge(slot_full[n % RING], 16 * (n // RING + 1))
                return unit_view(ring[:, n % RING, :], name)

            def three(a, b, ia, ib):
                return [(a[x][ia], b[y][ib]) for x, y in ((0, 0), (0, 1), (1, 0))]

            def x_tile(k, tokens=slice(0, L)):
                return (slice(0, P), k, tokens)

            def await_x(event, k):
                pe.wait_ge(xs_ready, event * KT + k + 1)

            def accumulate(out_ap, pairs, start=True, stop=True, shared=False):
                for n, (a, b) in enumerate(pairs):
                    last = nc.tensor.matmul(out_ap, a, b, start=start and n == 0,
                                            stop=stop and n == len(pairs) - 1, skip_group_check=shared)
                return last

            def sum_squares(l, part):
                g = Group(("rms", l, part))
                bank = begin(g)
                if part == 1:
                    pe.wait_ge(sum_ready, (l + 1) * (KT - 1))
                    nc.tensor.matmul(bank[:, 0:L], neg_ones[:, :], rstd[:, :], start=True, stop=True)\
                        .then_inc(work_done, 1)
                    return
                for k in range(KT):
                    pe.wait_ge(sq_ready, (2 * l + part) * KT + k + 1)
                    last = nc.tensor.matmul(bank[:, 0:L], neg_ones[:, :], xnT[:, k, :], start=k == 0,
                                            stop=k == KT - 1)
                last.then_inc(work_done, 1)

            pe.wait_ge(consts_made, 4)
            for t in range(KT * TT // 4):
                if t % (IN_BANKS // 2) == 0:
                    pe.wait_ge(x_loaded[t // (IN_BANKS // 2)], 16)
                g = Group(("in", t))
                bank = begin(g)
                for q in range(4):
                    k, tt = (4 * t + q) // TT, (4 * t + q) % TT
                    last = nc.tensor.transpose(bank[:, q * P:q * P + P], x_in[:, tt, k * P:k * P + P],
                                               ident[:, :])
                last.then_inc(work_done, 1)

            for l in range(DEPTH):
                sum_squares(l, 0)
                for kind, t in STEPS:
                    if kind in ("gelu", "softplus"):
                        continue
                    g = None if kind in NOT_WORK else Group((l, kind, t))
                    bank = None if g is None else begin(g)
                    if kind in ("q", "k", "u", "h", "b", "c"):
                        w = weights(l, f"{kind}{t}")
                        for k in range(KT):
                            if kind == "q" and t == 0:
                                await_x(3 * l, k)
                            for q in range(2):
                                pairs = three(w, x_parts, x_tile(k, slice(q * P, q * P + P)), x_tile(k))
                                last = accumulate(bank[:, q * L:q * L + L], pairs, start=k == 0 and q == 0,
                                                  stop=k == KT - 1, shared=True)
                        last.then_inc(work_done, 1)
                    elif kind == "v":
                        w = weights(l, f"v{t}")
                        for tt in range(TT):
                            pairs = []
                            for k in range(KT):
                                pairs += three(x_parts, w, x_tile(k, slice(tt * P, tt * P + P)), x_tile(k))
                            last = accumulate(bank[:, tt * UC:tt * UC + UC], pairs)
                        last.then_inc(work_done, 1)
                    elif kind == "z":
                        pe.wait_ge(q_ready, 2 * l + t + 1)
                        pe.wait_ge(k_ready, 2 * l + t + 1)
                        if 2 * l + t:
                            pe.wait_ge(attn_read, 2 * l + t)
                        for n in range(HB):
                            h = t * HB + n
                            r = slice(DH * (h % 2), DH * (h % 2) + DH)
                            nc.tensor.matmul(acc[:, n, 0:L], kT[r, h // 2, 0:P], qT[r, h // 2, :],
                                             start=True, stop=True, skip_group_check=True)
                            last = nc.tensor.matmul(acc[:, n, L:AW], kT[r, h // 2, P:L], qT[r, h // 2, P:L],
                                                    start=False, stop=True, skip_group_check=True)
                        last.then_inc(z_done, 1)
                    elif kind == "tail":
                        pe.wait_ge(stay_masked, 2 * l + t + 1)
                        for n in range(HB):
                            nc.tensor.matmul(acc[:, n, 0:AW], neg_incl[:, :], attn[:, n, :],
                                             start=False, stop=True, skip_group_check=True)
                            last = nc.tensor.matmul(acc[:, n, P:L], neg_ones[:, :], attn[:, n, L:AW],
                                                    start=False, stop=True, skip_group_check=True)
                        last.then_inc(tail_done, 1)
                    elif kind == "attend":
                        pe.wait_ge(w_masked, 2 * l + t + 1)
                        if t == 0:
                            pe.wait_ge(v_ready, 2 * l + 2)
                        for n in range(HB):
                            h = t * HB + n
                            r = slice(DH * (h % 2), DH * (h % 2) + DH)
                            hc = slice(h * DH, h * DH + DH)
                            nc.tensor.matmul(acc[r, n // 2, 0:L], v[:, 0, hc], attn[:, n, 0:L],
                                             start=True, stop=False, skip_group_check=True)
                            last = nc.tensor.matmul(acc[r, n // 2, P:L], v[:, 1, hc], attn[:, n, L:AW],
                                                    start=False, stop=True, skip_group_check=True)
                        last.then_inc(attn_done, 1)
                    elif kind == "bbT":
                        pe.wait_ge(bbp_ready, l + 1)
                        for q in range(4):
                            last = nc.tensor.transpose(bank[:, q * P:q * P + P],
                                                       bbp[:, q // 2, (q % 2) * P:(q % 2) * P + P], ident[:, :])
                        last.then_inc(work_done, 1)
                    elif kind == "bu":
                        if t == 0:
                            pe.wait_ge(bbT_ready, l + 1)
                            pe.wait_ge(u_ready, l + 1)
                        a, b = t // 4, 32 * (t % 4)
                        for q in range(2):
                            last = nc.tensor.matmul(bank[:, q * L:q * L + L], bbT[b:b + 32, 2 * q + a, :],
                                                    uT[b:b + 32, a, :], start=True, stop=True)
                        last.then_inc(work_done, 1)
                    elif kind == "ys":
                        pe.wait_ge(states_ready, l * SJ + t + 1)
                        if t == 0:
                            pe.wait_ge(c_ready, l + 1)
                        a, b = t // 4, 32 * (t % 4)
                        for q in range(2):
                            last = nc.tensor.matmul(ssm_y[b:b + 32, a, :], cblk[:, q, t, :], sring[:, t % 4, q, :],
                                                    start=q == 0, stop=q == 1)
                        last.then_inc(states_used, 1)
                    elif kind == "glu":
                        pe.wait_ge(glu_loaded, 16 * (l + 1))
                        pe.wait_ge(gelu_out, CT * (l + 1))
                        for q in range(CT):
                            last = accumulate(bank[:, q * L:q * L + L],
                                              [(wglu[:, k, q * P:q * P + P], uT[:, k, :]) for k in range(CT)])
                        last.then_inc(work_done, 1)
                    elif kind[0] == "g":
                        br = kind[1]
                        w = weights(l, f"{kind}{t // 2}")
                        tile = slice((t % 2) * P, (t % 2) * P + P)
                        pairs = []
                        for k in range(KT):
                            pairs += three(w, x_parts, x_tile(k, tile), x_tile(k))
                        accumulate(bank[:, 0:L], pairs)
                        if t == 0:
                            if br == "C":
                                pe.wait_ge(conv_ready, l + 1)
                            if br == "A":
                                pe.wait_ge(attn_read, 2 * l + 2)
                            if br == "B":
                                pe.wait_ge(yb_ready, l + 1)
                        act_in = {"A": qT, "B": uT, "C": hconv}[br]
                        pairs = []
                        for n in range((QW if br == "A" else CW) // UC):
                            if br == "A":
                                w = raw_weights(l, f"brA{n}")
                            else:
                                pe.wait_ge(br_full, 16 * (2 * l + "CB".index(br) + 1))
                                w = unit_view(br_slot[:, :], "br")
                            pairs += [(w[:, k, t * P:t * P + P], act_in[:, n * (UC // P) + k, :])
                                      for k in range(UC // P)]
                        accumulate(bank[:, L:2 * L], pairs).then_inc(work_done, 1)
                    elif kind == "wo":
                        w = weights(l, f"wo{t // 2}")
                        for k in range(KT):
                            if t == 0:
                                await_x(3 * l + 1, k)
                            last = accumulate(bank[:, 0:L],
                                              three(w, x_parts, x_tile(k, slice((t % 2) * P, (t % 2) * P + P)),
                                                    x_tile(k)), start=k == 0, stop=k == KT - 1)
                        last.then_inc(work_done, 1)

                sum_squares(l, 1)
                if l == 1:
                    continue

                def dense_down_product(c):
                    w = weights(0, f"D{c}")
                    pe.wait_ge(hid_split, (c + 1) * FT)
                    for f in range(FT):
                        for n in range(KT):
                            pairs = three(w, [h_parts[:, c % 2, q, f, :] for q in range(2)],
                                          (slice(0, P), f, slice(n * P, n * P + P)), slice(0, P))
                            last = accumulate(acc[:, n // 2, (n % 2) * L:(n % 2) * L + L], pairs,
                                              start=c == 0 and f == 0 and n % 2 == 0,
                                              stop=c == NHC - 1 and f == FT - 1, shared=True)
                    last.then_inc(down_done, 1)

                for c in range(NHC):
                    for q, name in enumerate((f"G{c}", f"U{c}")):
                        w = weights(0, name)
                        if q == 0:
                            banks = [begin(Group(("dense", c * FT + f))) for f in range(FT)]
                        order_kf = [(k, f) for k in range(KT) for f in range(FT)]
                        if c or q:
                            order_kf.sort(key=lambda kf: kf[1])
                        for k, f in order_kf:
                            if c == 0 and q == 0 and f == 0:
                                await_x(2, k)
                            last = accumulate(banks[f][:, q * L:q * L + L],
                                              three(w, x_parts, x_tile(k, slice(f * P, f * P + P)), x_tile(k)),
                                              start=k == 0, stop=k == KT - 1)
                            if q == 1 and k == KT - 1:
                                last.then_inc(work_done, 1)
                        if q == 0:
                            last.then_inc(half_done, 1)
                    if c:
                        dense_down_product(c - 1)
                dense_down_product(NHC - 1)

            bank = begin(Group(("router", 0)))
            pe.wait_ge(wr_loaded, 16)
            for k in range(KT):
                pe.wait_ge(xn_ready, (2 * DEPTH - 1) * KT + k + 1)
                for t in range(TT):
                    last = accumulate(bank[:, t * NE:t * NE + NE], [(xnT[:, k, t * P:t * P + P], wr[:, k, :])],
                                      start=k == 0 and t == 0, stop=k == KT - 1, shared=True)
            last.then_inc(work_done, 1)
            for t in range(4 * TT):
                bank = begin(Group(("tok", t)))
                src = xnT if t < 2 * TT else hT
                tt, half = (t % (2 * TT)) // 2, t % 2
                for q in range(4):
                    last = nc.tensor.transpose(bank[:, q * P:q * P + P],
                                               src[:, half * 4 + q, tt * P:tt * P + P], ident[:, :])
                last.then_inc(work_done, 1)
            bank = begin(Group(("rank", 0)))
            pe.wait_ge(chosen_ready, 1)
            for t in range(TT):
                pairs = [(neg_ones[:, :], chosen[:, s, :]) for s in range(t)]
                accumulate(bank[:, t * NE:t * NE + NE], pairs + [(neg_incl[:, :], rest[:, t, :]),
                                                                 (neg_ones[:, :], chosen[:, t, :])])
            accumulate(bank[:, TT * NE:TT * NE + NE], [(neg_ones[:, :], chosen[:, t, :]) for t in range(TT)])\
                .then_inc(work_done, 1)

            def gather(key, item, half):
                bank = begin(Group((key, half), item), item)
                for q in range(HALF):
                    d = (half * HALF + q) * P
                    last = accumulate(bank[:, q * SLOTS:q * SLOTS + SLOTS],
                                      [(xn_tok[:, t, d:d + P], pick[:, t, :]) for t in range(TT)])
                last.then_inc(work_done, 1)

            pe.wait_ge(tok_ready, 2 * TT)
            pe.wait_ge(pick_ready, 1)
            for half in range(2):
                gather("gather0", None, half)
            pe.wait_ge(items_ready, 1)
            n_items = pe.value_load(items[0:1, CAND + 1:CAND + 2], min_val=NE, max_val=CAND)
            with pe.Fori(0, n_items) as i:
                pe.wait_ge(xe_ready, i * 2 + 2)

                def turn_weights():
                    pe.wait_ge(wpick_ready, i + 1)
                    for t in range(TT):
                        last = nc.tensor.transpose(acc[0:SLOTS, 2, t * P:t * P + P], wpick[:, t, :], ident[:, :])
                    last.then_inc(wpick_turned, 1)

                def project(kind, c):
                    bank = begin(Group((kind, c), i), i)
                    for half in range(2):
                        w = item_weights(f"{kind.upper()}{2 * c + half}", i)
                        for k in range(HALF):
                            pairs = three(xe_parts, w, (slice(0, P), half * HALF + k, slice(0, SLOTS)),
                                          (slice(0, P), k, slice(0, CW2)))
                            last = accumulate(bank[0:SLOTS, :], pairs, start=half == 0 and k == 0,
                                              stop=half == 1 and k == HALF - 1)
                        last.then_inc(work_done if half else half_done, 1)

                def turn(c):
                    bank = begin(Group(("t", c), i), i)
                    pe.wait_ge(erow_ready, i * NCH + (c + 1))
                    for q in range(HT):
                        last = nc.tensor.transpose(bank[:, q * SLOTS:q * SLOTS + SLOTS],
                                                   erow[0:SLOTS, q * P:q * P + P], ident[0:SLOTS, 0:SLOTS])
                    last.then_inc(work_done, 1)

                def down(c):
                    pe.wait_ge(eh_ready, i * NCH + (c + 1))
                    for n in range(2):
                        w = item_weights(f"D{2 * c + n}", i)
                        for f in range(FT):
                            for half in range(2):
                                pairs = three(eh_parts, w, (slice(0, P), n * FT + f, slice(0, SLOTS)),
                                              (slice(0, P), f, slice(half * 512, half * 512 + 512)))
                                last = accumulate(acc[0:SLOTS, half, :], pairs,
                                                  start=c == 0 and n == 0 and f == 0,
                                                  stop=c == NCH - 1 and n == 1 and f == FT - 1, shared=True)
                        last.then_inc(down_done, 1)

                for c in range(NCH):
                    project("g", c)
                    if c == 0:
                        turn_weights()
                    else:
                        turn(c - 1)
                    project("u", c)
                    if c:
                        down(c - 1)
                pe.wait_ge(pick_ready, i + 2)
                gather("gather", i, 0)
                turn(NCH - 1)
                gather("gather", i, 1)
                down(NCH - 1)
                pe.wait_ge(combine_ready, i + 1)
                for t in range(2 * TT):
                    bank = begin(Group(("comb", t), i), i)
                    half, tt = t // TT, t % TT
                    if tt == 0:
                        pe.wait_ge(y_ready, i * 2 + (half + 1))
                    nc.tensor.matmul(bank[:, :], combine[0:SLOTS, tt * P:tt * P + P],
                                     y_tok[0:SLOTS, half * 512:half * 512 + 512], start=True, stop=True)\
                        .then_inc(work_done, 1)

        @block.scalar
        def _(act):
            chain = [0]

            def link(ins):
                chain[0] += 1
                ins.then_inc(act_chain, 1)
                act.wait_ge(act_chain, chain[0])

            def arrived(g):
                act.wait_ge(work_done, g.done)
                return work[:, g.bank, :]

            act.dma_start(lam[:, 0, :], lam_re.rearrange("p l j -> p (l j)")).then_inc(params_loaded, 16)
            act.dma_start(lam[:, 1, :], lam_im.rearrange("p l j -> p (l j)")).then_inc(params_loaded, 16)
            for par in range(2):
                src = log_dt[par:par + 1].rearrange("q l j -> q (l j)").to_broadcast([P // 2, DEPTH * SJ])
                act.dma_start(logdt[par * (P // 2):par * (P // 2) + P // 2, :], src).then_inc(params_loaded, 16)
            for l in range(DEPTH):
                act.dma_start(gains[:, 2 * l, :], gain_mix[l]).then_inc(params_loaded, 16)
                act.dma_start(gains[:, 2 * l + 1, :], gain_ffn[l]).then_inc(params_loaded, 16)
            act.dma_start(dskip[:, :, :], ssm_d).then_inc(params_loaded, 16)
            act.dma_start(convw[:, :, :, :], conv_w).then_inc(params_loaded, 16)
            act.dma_start(wr[:, :, :], rows(w_router[0])).then_inc(wr_loaded, 16)

            def split(s):
                n = STREAM.index(SPLIT[s])
                act.wait_ge(slot_full[n % RING], 16 * (n // RING + 1))
                if s >= PARTS:
                    act.wait_ge(*used_up(*SPLIT[s - PARTS]))
                nc.scalar.activation(parts[:, s % PARTS, 0, :], ring[:, n % RING, :], ACT.Copy)\
                    .then_inc(hi_ready, 1)

            splits = Splitter(split)

            def x_high(src, source, value):
                for k in range(KT):
                    act.wait_ge(source, value(k))
                    nc.scalar.activation(x_parts[0][:, k, :], src[:, k, :], ACT.Copy).then_inc(xs_hi_ready, 1)

            def square(l, part, k):
                if part == 1:
                    act.wait_ge(h_ready, H_MIXED[l] + k + 1)
                else:
                    act.wait_ge(h_ready, H_MIXED[l] - 4 + k // 2 + 1)
                nc.scalar.activation(xnT[:, k, :], hT[:, k, :], ACT.Square).then_inc(sq_ready, 1)

            def root_mean_square(l, part):
                bank = arrived(Group(("rms", l, part)))
                nc.scalar.activation(rstd[:, :], bank[:, 0:L], ACT.Ln, bias=bias[:, 0:1], scale=-1.0 / D)\
                    .then_inc(rms_read, 1)
                act.wait_ge(rms_read, 2 * l + part + 1)
                nc.scalar.activation(rstd[:, :], rstd[:, :], ACT.Exp, scale=-0.5).then_inc(rstd_ready, 1)

            act.wait_ge(consts_made, 4)
            act.preload_act_table_set("natural_log_exp_and_others")
            for k in range(KT):
                square(0, 0, k)
            splits.upto_first(1)
            root_mean_square(0, 0)
            x_high(xnT, xn_ready, lambda k: k + 1)
            splits.upto_first(AHEAD)
            act.wait_ge(params_loaded, 16 * PARAMS)
            nc.scalar.activation(dt, logdt[:, :], ACT.Exp).then_inc(dt_ready, 1)
            act.wait_ge(angle_ready, 1)
            nc.scalar.activation(mag, decay, ACT.Exp).then_inc(sincos_ready, 1)
            nc.scalar.activation(sin1, reduced, ACT.Sin).then_inc(sincos_ready, 1)
            nc.scalar.activation(cos1, upright, ACT.Sin).then_inc(sincos_ready, 1)
            act.preload_act_table_set("natural_log_exp_and_others")

            for l in range(DEPTH):
                if l:
                    for k in range(KT):
                        square(l, 0, k)
                    root_mean_square(l, 0)
                    x_high(xnT, xn_ready, lambda k: 2 * l * KT + k + 1)
                for kind, t in STEPS:
                    if (kind, t) == ("wo", 0):
                        act.wait_ge(work_done, Group((l, "gB", KT - 1)).done)
                        x_high(merged, merged_ready, lambda k: l * KT + k + 1)
                    if unit_of(kind, t) is not None:
                        splits.upto(l, unit_of(kind, t))
                    if kind == "q":
                        bank = arrived(Group((l, kind, t)))
                        nc.scalar.activation(qT[:, 2 * t:2 * t + 2, :].rearrange("p t n -> p (t n)"), bank[:, :],
                                             ACT.Copy, scale=SCALE).then_inc(q_ready, 1)
                    elif kind in ("h", "b"):
                        bank = arrived(Group((l, kind, t)))
                        dst = hconv if kind == "h" else bconv
                        nc.scalar.activation(dst[:, :, :].rearrange("p t n -> p (t n)"), bank[:, :], ACT.Copy)\
                            .then_inc(h_conv_ready if kind == "h" else b_conv_ready, 1)
                    elif kind == "bbT":
                        bank = arrived(Group((l, kind, t)))
                        nc.scalar.activation(bbT[:, :, :].rearrange("p t n -> p (t n)"), bank[:, :], ACT.Copy)\
                            .then_inc(bbT_ready, 1)
                    elif kind == "z":
                        act.wait_ge(z_done, 2 * l + t + 1)
                        link(nc.scalar.activation(attn[:, :, :], attn_z, ACT.Abs))
                        act.preload_act_table_set("natural_log_exp_and_others")
                        link(nc.scalar.activation(attn[:, :, :], attn[:, :, :], ACT.Exp, scale=-1.0))
                        nc.scalar.activation(attn[:, :, :], attn[:, :, :], ACT.Ln, bias=bias[:, 1:2])\
                            .then_inc(log_ready, 1)
                    elif kind == "tail":
                        act.wait_ge(tail_done, 2 * l + t + 1)
                        nc.scalar.activation(attn[:, :, :], attn_z, ACT.Exp).then_inc(w_ready, 1)
                    elif kind == "gelu":
                        for a in range(CT):
                            act.wait_ge(gelu_in, CT * l + a + 1)
                            nc.scalar.activation(uT[:, a, :], uT[:, a, :], ACT.Gelu_apprx_tanh)\
                                .then_inc(gelu_out, 1)
                    elif kind == "glu":
                        bank = arrived(Group((l, kind, t)))
                        nc.scalar.activation(bconv[:, :, :].rearrange("p t n -> p (t n)"), bank[:, :],
                                             ACT.Sigmoid).then_inc(glu_ready, 1)
                    elif kind in ("gA", "gB", "gC"):
                        n = gate_number(l, kind[1], t)
                        bank = arrived(Group((l, kind, t)))
                        if n >= 2:
                            act.wait_ge(gate_used, n - 1)
                        nc.scalar.activation(sig[:, n % 2, :], bank[:, 0:L], ACT.Sigmoid).then_inc(sig_ready, 1)
                    elif kind == "wo":
                        if t == 0:
                            act.preload_act_table_set("natural_log_exp_and_others")
                        else:
                            square(l, 1, t - 1)
                square(l, 1, KT - 1)
                root_mean_square(l, 1)
                if l == 0:
                    x_high(xnT, xn_ready, lambda k: KT + k + 1)

                    def hidden_high(n):
                        c, f = n // FT, n % FT
                        act.wait_ge(hid_ready, n + 1)
                        if c >= 2:
                            act.wait_ge(down_done, c - 1)
                        nc.scalar.activation(h_parts[:, c % 2, 0, f, :], hid[:, n % 2, :], ACT.Copy)\
                            .then_inc(hid_hi_ready, 1)

                    for c in range(NHC):
                        splits.upto(0, f"G{c}")
                        if c:
                            hidden_high(c * FT - 1)
                        splits.upto(0, f"U{c}")
                        for n in range(c * FT, c * FT + FT):
                            if n > c * FT:
                                hidden_high(n - 1)
                            bank = arrived(Group(("dense", n)))
                            if n >= 2:
                                act.wait_ge(hid_ready, n - 1)
                            nc.scalar.activation(sig[:, n % 2, :], bank[:, 0:L], ACT.Silu).then_inc(silu_ready, 1)
                        if c:
                            splits.upto(0, f"D{c - 1}")
                    hidden_high(DENSE_TILES - 1)
                    splits.upto(0, f"D{NHC - 1}")

            def split_first(j):
                n = len(STREAM) + j
                act.wait_ge(slot_full[n % RING], 16 * (n // RING + 1))
                act.wait_ge(*used_up(*SPLIT[S0 + j - PARTS]))
                nc.scalar.activation(parts[:, (S0 + j) % PARTS, 0, :], ring[:, n % RING, :], ACT.Copy)\
                    .then_inc(hi_ready, 1)

            for j in range(FIRST):
                split_first(j)
            act.dma_start(g_row, gain_final[0:1, :].to_broadcast([P, D])).then_inc(row_loaded, 16)
            for t in range(2 * TT):
                bank = arrived(Group(("tok", t)))
                nc.scalar.activation(xn_tok[:, t // 2, (t % 2) * 512:(t % 2) * 512 + 512], bank[:, :], ACT.Copy)\
                    .then_inc(tok_ready, 1)
            for t in range(2 * TT):
                bank = arrived(Group(("tok", 2 * TT + t)))
                nc.scalar.activation(h_tok[:, t // 2, (t % 2) * 512:(t % 2) * 512 + 512], bank[:, :], ACT.Copy)\
                    .then_inc(h_tok_ready, 1)
            act.wait_ge(diff_ready, 1)
            nc.scalar.activation(stat[:, :, 3:4], stat[:, :, 2:3], ACT.Exp).then_inc(expd_ready, 1)

            def move_tokens(key, item, half):
                bank = arrived(Group((key, half), item))
                nc.scalar.activation(xe_parts[0][:, half * HALF:half * HALF + HALF, :]
                                     .rearrange("p t n -> p (t n)"), bank[:, 0:HALF * SLOTS], ACT.Copy)\
                    .then_inc(xe_hi_ready, 1)

            for half in range(2):
                move_tokens("gather0", None, half)
            act.wait_ge(items_ready, 1)
            n_items = act.value_load(items[0:1, CAND + 1:CAND + 2], min_val=NE, max_val=CAND)

            def chunk_high(c, i):
                bank = arrived(Group(("t", c), i))
                nc.scalar.activation(eh_parts[0].rearrange("p t n -> p (t n)"), bank[:, 0:HT * SLOTS], ACT.Copy)\
                    .then_inc(eh_hi_ready, 1)

            act.preload_act_table(ACT.Silu)
            with act.Fori(0, n_items) as i:
                def split_item(j):
                    n = len(STREAM) + j
                    act.wait_ge(slot_full[n % RING], i * (16 * IU // RING) + 16 * (n // RING + 1))
                    if j >= PARTS:
                        act.wait_ge(*item_used_up(EXPERT[j - PARTS], i))
                    else:
                        act.wait_ge(down_done, i * NHC + (NHC - PARTS + j + 1))
                    nc.scalar.activation(parts[:, (S0 + j) % PARTS, 0, :], ring[:, n % RING, :], ACT.Copy)\
                        .then_inc(hi_ready, 1)

                splits = ItemSplitter(split_item)
                for c in range(NCH):
                    splits.upto(f"G{2 * c}")
                    splits.upto(f"G{2 * c + 1}")
                    bank = arrived(Group(("g", c), i))
                    if c:
                        act.wait_ge(erow_ready, i * NCH + c)
                    nc.scalar.activation(esilu[0:SLOTS, :], bank[0:SLOTS, :], ACT.Silu).then_inc(esilu_ready, 1)
                    if c:
                        chunk_high(c - 1, i)
                    if c == 1:
                        act.wait_ge(wpick_turned, i + 1)
                        nc.scalar.activation(combine[0:SLOTS, :], acc[0:SLOTS, 2, 0:L], ACT.Copy)\
                            .then_inc(combine_ready, 1)
                    splits.upto(f"U{2 * c}")
                    splits.upto(f"U{2 * c + 1}")
                    if c:
                        splits.upto(f"D{2 * c - 2}")
                        splits.upto(f"D{2 * c - 1}")
                move_tokens("gather", i, 0)
                chunk_high(NCH - 1, i)
                move_tokens("gather", i, 1)
                splits.upto_first(IU + FIRST)
                act.wait_ge(down_done, i * NHC + 2 * NHC)
                for half in range(2):
                    nc.scalar.activation(y_tok[0:SLOTS, half * 512:half * 512 + 512], acc[0:SLOTS, half, :],
                                         ACT.Copy).then_inc(y_ready, 1)
            act.preload_act_table_set("natural_log_exp_and_others")
            act.wait_ge(h_tok_ready, n_items * 2 * TT + 2 * TT)
            for t in range(TT):
                last = nc.scalar.activation(xn_tok[:, t, :], h_tok[:, t, :], ACT.Square,
                                            accum_out=sumsq[:, t:t + 1])
                link(last)
            link(nc.scalar.activation(sumsq[:, :], sumsq[:, :], ACT.Ln, bias=bias[:, 0:1], scale=1.0 / D))
            nc.scalar.activation(sumsq[:, :], sumsq[:, :], ACT.Exp, scale=-0.5).then_inc(final_rstd, 1)

        @block.vector
        def _(dve):
            chain = [0]

            def link(ins):
                chain[0] += 1
                ins.then_inc(dve_chain, 1)
                dve.wait_ge(dve_chain, chain[0])

            def arrived(g):
                dve.wait_ge(work_done, g.done)
                return work[:, g.bank, :]

            tt, ts, stt = nc.vector.tensor_tensor, nc.vector.tensor_scalar, nc.vector.scalar_tensor_tensor
            for t in range(IN_BANKS):
                bank = arrived(Group(("in", t)))
                nc.vector.tensor_copy(hT[:, 2 * t:2 * t + 2, :].rearrange("p t n -> p (t n)"), bank[:, :])\
                    .then_inc(h_ready, 1)

            def split(s):
                n = STREAM.index(SPLIT[s])
                dve.wait_ge(hi_ready, s + 1)
                tt(parts[:, s % PARTS, 1, :], ring[:, n % RING, :], parts[:, s % PARTS, 0, :].bitcast(F32),
                   ALU.subtract).then_inc(lo_ready, 1)

            splits = Splitter(split)

            def x_rest(event, src, k):
                dve.wait_ge(xs_hi_ready, event * KT + k + 1)
                tt(x_parts[1][:, k, :], src[:, k, :], x_parts[0][:, k, :].bitcast(F32), ALU.subtract)\
                    .then_inc(xs_ready, 1)

            def normalise(l, part):
                n = 2 * l + part
                dve.wait_ge(rstd_ready, n + 1)
                if n == 0:
                    dve.wait_ge(params_loaded, 16 * PARAMS)
                for k in range(KT + 1):
                    if k < KT:
                        stt(xnT[:, k, :], hT[:, k, :], gains[:, n, k:k + 1], rstd[:, :], ALU.mult, ALU.mult)\
                            .then_inc(xn_ready, 1)
                    if k and n < 2 * DEPTH - 1:
                        x_rest(3 * l + 2 * part, xnT, k - 1)

            splits.upto_first(1)
            normalise(0, 0)
            splits.upto_first(AHEAD)

            dve.wait_ge(dt_ready, 1)
            link(ts(lr, lam[:, 0, :], -1e-4, None, ALU.min))
            link(tt(decay, lr, dt, ALU.mult))
            link(tt(angle, lam[:, 1, :], dt, ALU.mult))
            magic = 1.5 * 2.0 ** 23
            link(ts(turns, angle, 1.0 / (2 * math.pi), magic, ALU.mult, ALU.add))
            link(ts(turns, turns, -magic, None, ALU.add))
            two_pi = [6.28125, 0.0019350051879882812, 3.0199159819567633e-07]
            link(stt(reduced, turns, -two_pi[0], angle, ALU.mult, ALU.add))
            link(stt(reduced, turns, -two_pi[1], reduced, ALU.mult, ALU.add))
            link(stt(reduced, turns, -two_pi[2], reduced, ALU.mult, ALU.add))
            link(ts(reduced, reduced, 3.1415925, -3.1415925, ALU.min, ALU.max))
            link(ts(upright, reduced, -1.0, None, ALU.mult))
            link(tt(upright, reduced, upright, ALU.max))
            ts(upright, upright, -1.0, math.pi / 2, ALU.mult, ALU.add).then_inc(angle_ready, 1)
            li = lam[:, 1, :]
            link(tt(den, lr, lr, ALU.mult))
            link(tt(tmp1, li, li, ALU.mult))
            link(tt(den, den, tmp1, ALU.add))
            link(nc.vector.reciprocal(den, den))
            dve.wait_ge(sincos_ready, 3)
            link(tt(nr, mag, cos1, ALU.mult))
            link(ts(nr, nr, -1.0, None, ALU.add))
            link(tt(tmp2, mag, sin1, ALU.mult))
            link(tt(f_re, nr, lr, ALU.mult))
            link(tt(tmp1, tmp2, li, ALU.mult))
            link(tt(f_re, f_re, tmp1, ALU.add))
            link(tt(f_re, f_re, den, ALU.mult))
            link(tt(f_im, tmp2, lr, ALU.mult))
            link(tt(tmp1, nr, li, ALU.mult))
            link(tt(f_im, f_im, tmp1, ALU.subtract))
            tt(f_im, f_im, den, ALU.mult).then_inc(f_ready, 1)

            def add_square(l, k):
                dve.wait_ge(sq_ready, (2 * l + 1) * KT + k + 1)
                if k >= 2:
                    dve.wait_ge(sum_ready, l * (KT - 1) + k - 1)
                tt(rstd[:, :], xnT[:, 0, :] if k == 1 else rstd[:, :], xnT[:, k, :], ALU.add)\
                    .then_inc(sum_ready, 1)

            prod = vtmp[:, 0, :]
            for l in range(DEPTH):
                if l:
                    normalise(l, 0)
                for kind, t in STEPS:
                    if (kind, t) == ("wo", 0):
                        for k in range(KT):
                            x_rest(3 * l + 1, merged, k)
                    if unit_of(kind, t) is not None:
                        splits.upto(l, unit_of(kind, t))
                    if kind == "k":
                        bank = arrived(Group((l, kind, t)))
                        nc.vector.tensor_copy(kT[:, 2 * t:2 * t + 2, :].rearrange("p t n -> p (t n)"), bank[:, :])\
                            .then_inc(k_ready, 1)
                    elif kind == "v":
                        bank = arrived(Group((l, kind, t)))
                        nc.vector.tensor_copy(v[:, :, t * UC:t * UC + UC],
                                              bank[:, :].rearrange("p (t n) -> p t n", n=UC)).then_inc(v_ready, 1)
                    elif kind == "u":
                        bank = arrived(Group((l, kind, t)))
                        nc.vector.tensor_copy(uT[:, :, :].rearrange("p t n -> p (t n)"), bank[:, :])\
                            .then_inc(u_ready, 1)
                    elif kind == "softplus":
                        dve.wait_ge(log_ready, 2 * l + t + 1)
                        stt(attn[:, :, :], attn_z, 0.0, attn[:, :, :], ALU.max, ALU.add).then_inc(stay_ready, 1)
                    elif kind == "attend":
                        dve.wait_ge(attn_done, 2 * l + t + 1)
                        nc.vector.tensor_copy(qT[:, 2 * t:2 * t + 2, :], acc[:, 0:2, 0:L]).then_inc(attn_read, 1)
                    elif kind == "c":
                        bank = arrived(Group((l, kind, t)))
                        dve.wait_ge(h_conv_ready, l + 1)
                        tt(uconv[:, :, 2:L + 2], bank[:, :].rearrange("p (t n) -> p t n", n=L), hconv[:, :, :],
                           ALU.mult).then_inc(conv_u_ready, 1)
                        dve.wait_ge(conv_u_ready, l + 1)
                        dve.wait_ge(consts_made, 4)
                        for a in range(CT):
                            link(ts(hconv[:, a, :], uconv[:, a, 0:L], convw[:, l, 0, a:a + 1], None, ALU.mult))
                        for tap in (1, 2):
                            for a in range(CT):
                                link(stt(hconv[:, a, :], uconv[:, a, tap:tap + L], convw[:, l, tap, a:a + 1],
                                         hconv[:, a, :], ALU.mult, ALU.add))
                        dve.wait_ge(b_conv_ready, l + 1)
                        tt(hconv[:, :, :], hconv[:, :, :], bconv[:, :, :], ALU.mult).then_inc(conv_ready, 1)
                    elif kind == "bu":
                        n = l * SJ + t
                        bank = arrived(Group((l, kind, t)))
                        dve.wait_ge(tables_ready, l + 1)
                        if t >= 4:
                            dve.wait_ge(states_used, n - 3)
                        re, im = bank[:, 0:L], bank[:, L:2 * L]
                        s_re, s_im = sring[:, t % 4, 0, :], sring[:, t % 4, 1, :]
                        tt(s_re, re, cosT[:, t, :], ALU.mult)
                        tt(s_im, im, cosT[:, t, :], ALU.mult)
                        tt(vtmp[:, 0, :], im, sinT[:, t, :], ALU.mult)
                        tt(vtmp[:, 1, :], re, sinT[:, t, :], ALU.mult).then_inc(bu_read, 1)
                        dve.wait_ge(bu_read, n + 1)
                        link(tt(s_re, s_re, vtmp[:, 0, :], ALU.add))
                        link(tt(s_im, s_im, vtmp[:, 1, :], ALU.subtract))
                        step = mag[:, n:n + 1].to_broadcast([P, L])
                        for s in (s_re, s_im):
                            nc.vector.tensor_tensor_scan(s, step, s, 0.0, ALU.mult, ALU.add).then_inc(scanned, 1)
                    elif kind == "gelu":
                        dve.wait_ge(states_used, l * SJ + SJ)
                        for a in range(CT):
                            stt(uT[:, a, :], uT[:, a, :], dskip[:, l, a:a + 1], ssm_y[:, a, :], ALU.mult, ALU.add)\
                                .then_inc(gelu_in, 1)
                    elif kind == "glu":
                        dve.wait_ge(glu_ready, l + 1)
                        tt(uT[:, :, :], uT[:, :, :], bconv[:, :, :], ALU.mult).then_inc(yb_ready, 1)
                    elif kind in ("gA", "gB", "gC"):
                        n = gate_number(l, kind[1], t)
                        bank = arrived(Group((l, kind, t)))
                        dve.wait_ge(sig_ready, n + 1)
                        dst = merged[:, t, :] if kind == "gC" else prod
                        tt(dst, sig[:, n % 2, :], bank[:, L:2 * L], ALU.mult).then_inc(gate_used, 1)
                        if kind != "gC":
                            dve.wait_ge(gate_used, n + 1)
                            last = tt(merged[:, t, :], merged[:, t, :], prod, ALU.add)
                            if kind == "gA":
                                link(last)
                            else:
                                last.then_inc(merged_ready, 1)
                                dve.wait_ge(merged_ready, l * KT + t + 1)
                    elif kind == "wo":
                        bank = arrived(Group((l, kind, t)))
                        tt(hT[:, t, :], hT[:, t, :], bank[:, 0:L], ALU.add).then_inc(h_ready, 1)
                        if t >= 2:
                            add_square(l, t - 1)
                        if t == KT - 1:
                            add_square(l, t)
                normalise(l, 1)
                if l == 0:
                    def hidden_rest(n):
                        c, f = n // FT, n % FT
                        dve.wait_ge(hid_hi_ready, n + 1)
                        tt(h_parts[:, c % 2, 1, f, :], hid[:, n % 2, :], h_parts[:, c % 2, 0, f, :].bitcast(F32),
                           ALU.subtract).then_inc(hid_split, 1)

                    for c in range(NHC):
                        splits.upto(0, f"G{c}")
                        if c:
                            hidden_rest(c * FT - 1)
                        splits.upto(0, f"U{c}")
                        for n in range(c * FT, c * FT + FT):
                            if n > c * FT:
                                hidden_rest(n - 1)
                            bank = arrived(Group(("dense", n)))
                            dve.wait_ge(silu_ready, n + 1)
                            if n >= 2:
                                dve.wait_ge(hid_split, n - 1)
                            tt(hid[:, n % 2, :], sig[:, n % 2, :], bank[:, L:2 * L], ALU.mult)\
                                .then_inc(hid_ready, 1)
                        if c:
                            splits.upto(0, f"D{c - 1}")
                    hidden_rest(DENSE_TILES - 1)
                    splits.upto(0, f"D{NHC - 1}")
                    dve.wait_ge(down_done, NHC)
                    for b in range(4):
                        tt(hT[:, 2 * b:2 * b + 2, :].rearrange("p t n -> p (t n)"),
                           hT[:, 2 * b:2 * b + 2, :].rearrange("p t n -> p (t n)"), acc[:, b, :], ALU.add)\
                            .then_inc(h_ready, 1)

            def split_any(j, i):
                dve.wait_ge(hi_ready, i * IU + (S0 + j + 1))
                tt(parts[:, (S0 + j) % PARTS, 1, :], raw_unit(j),
                   parts[:, (S0 + j) % PARTS, 0, :].bitcast(F32), ALU.subtract).then_inc(lo_ready, 1)

            split_any(0, 0)
            bank = arrived(Group(("router", 0)))
            nc.vector.tensor_copy(logits[:, :, :].rearrange("p t n -> p (t n)"), bank[:, 0:TT * NE])\
                .then_inc(logits_ready, 1)
            dve.wait_ge(logits_ready, 1)
            for t in range(TT):
                link(nc.vector.max(stat[:, t, :], logits[:, t, :]))
                link(ts(order[:, t, :], slot_no[:, 0:NE], -1.0, float(NE), ALU.mult, ALU.add))
            for t in range(TT):
                link(stt(mask1[:, t, :], logits[:, t, :], stat[:, t, 0:1], order[:, t, :], ALU.is_equal, ALU.mult))
                link(nc.vector.reduce_max(stat[:, t, 7:8], mask1[:, t, :], AX.X))
                link(ts(mask1[:, t, :], mask1[:, t, :], stat[:, t, 7:8], None, ALU.is_equal))
                link(stt(mask2[:, t, :], logits[:, t, :], stat[:, t, 1:2], order[:, t, :], ALU.is_equal, ALU.mult))
                link(ts(chosen[:, t, :], mask1[:, t, :], -1.0, 1.0, ALU.mult, ALU.add))
                link(tt(mask2[:, t, :], mask2[:, t, :], chosen[:, t, :], ALU.mult))
                link(nc.vector.reduce_max(stat[:, t, 7:8], mask2[:, t, :], AX.X))
                link(ts(mask2[:, t, :], mask2[:, t, :], stat[:, t, 7:8], None, ALU.is_equal))
                link(tt(chosen[:, t, :], mask1[:, t, :], mask2[:, t, :], ALU.add))
            ts(rest[:, :, :], chosen[:, :, :], -1.0, None, ALU.mult).then_inc(chosen_ready, 1)
            for j in range(1, FIRST):
                split_any(j, 0)
            tt(stat[:, :, 2:3], stat[:, :, 1:2], stat[:, :, 0:1], ALU.subtract).then_inc(diff_ready, 1)
            bank = arrived(Group(("rank", 0)))
            nc.vector.tensor_copy(neg_rank[:, :, :].rearrange("p t n -> p (t n)"), bank[:, 0:(TT + 1) * NE])\
                .then_inc(rank_read, 1)
            dve.wait_ge(rank_read, 1)
            link(stt(order[:, :, :], neg_rank[:, 0:TT, :], -1.0, rest[:, :, :], ALU.add, ALU.mult))
            for r in range(ROUNDS):
                link(ts(rank_c[:, :, r * NE:r * NE + NE], order[:, :, :], -1.0 - SLOTS * r, None, ALU.add))

            def build_pick(c):
                for t in range(TT):
                    last = ts(pick[:, t, :], slot_no[:, :], rank_c[:, t, c], None, ALU.is_equal)
                last.then_inc(pick_ready, 1)

            def build_wpick(c):
                for t in range(TT):
                    last = ts(wpick[:, t, :], slot_no[:, :], rank_c[:, t, c], wgt_c[:, t, c], ALU.is_equal,
                              ALU.mult)
                last.then_inc(wpick_ready, 1)

            build_pick(slice(0, 1))
            for r in range(1, ROUNDS):
                link(ts(active[:, (r - 1) * NE:r * NE], neg_rank[:, TT, :], float(-SLOTS * r), None, ALU.is_lt))
            link(nc.vector.tensor_tensor_scan(place, active, active, 0.0, ALU.add, ALU.max))
            link(tt(value, active, slot_no[:, NE:CAND], ALU.mult))
            link(tt(grid[:, :, :], place.unsqueeze(1).to_broadcast([P, XC, XC]),
                    slot_no[:, 1:XC + 1].unsqueeze(2).to_broadcast([P, XC, XC]), ALU.is_equal))
            link(tt(grid[:, :, :], grid[:, :, :], value.unsqueeze(1).to_broadcast([P, XC, XC]), ALU.mult))
            link(nc.vector.reduce_sum(listf[:, NE:CAND], grid[:, :, :], AX.X))
            link(nc.vector.tensor_copy(listf[:, 0:NE], slot_no[:, 0:NE]))
            link(ts(listf[:, CAND:CAND + 1], slot_no[:, 0:1], 0.0, None, ALU.mult))
            link(ts(listf[:, CAND + 1:CAND + 2], place[:, XC - 1:XC], float(NE), None, ALU.add))
            nc.vector.tensor_copy(items[:, :], listf).then_inc(items_ready, 1)

            def token_rests(key, item, half):
                bank = work[:, Group((key, half), item).bank, 0:HALF * SLOTS]
                dve.wait_ge(xe_hi_ready, half + 1 if item is None else item * 2 + (3 + half))
                cut = slice(half * HALF, half * HALF + HALF)
                tt(xe_parts[1][:, cut, :].rearrange("p t n -> p (t n)"), bank,
                   xe_parts[0][:, cut, :].rearrange("p t n -> p (t n)").bitcast(F32), ALU.subtract)\
                    .then_inc(xe_ready, 1)

            def chunk_rest(c, i):
                bank = work[:, Group(("t", c), i).bank, 0:HT * SLOTS]
                dve.wait_ge(eh_hi_ready, i * NCH + (c + 1))
                tt(eh_parts[1].rearrange("p t n -> p (t n)"), bank,
                   eh_parts[0].rearrange("p t n -> p (t n)").bitcast(F32), ALU.subtract).then_inc(eh_ready, 1)

            for half in range(2):
                token_rests("gather0", None, half)
            dve.wait_ge(expd_ready, 1)
            link(ts(stat[:, :, 4:5], stat[:, :, 3:4], 1.0, None, ALU.add))
            link(nc.vector.reciprocal(stat[:, :, 5:6], stat[:, :, 4:5]))
            link(tt(stat[:, :, 6:7], stat[:, :, 3:4], stat[:, :, 5:6], ALU.mult))
            for t in range(TT):
                link(ts(mask1[:, t, :], mask1[:, t, :], stat[:, t, 5:6], None, ALU.mult))
                for r in range(ROUNDS):
                    link(stt(wgt_c[:, t, r * NE:r * NE + NE], mask2[:, t, :], stat[:, t, 6:7], mask1[:, t, :],
                             ALU.mult, ALU.add))
            build_wpick(slice(0, 1))
            dve.wait_ge(items_ready, 1)
            n_items = dve.value_load(items[0:1, CAND + 1:CAND + 2], min_val=NE, max_val=CAND)
            with dve.Fori(0, n_items) as i:
                splits = ItemSplitter(lambda j: split_any(j, i))
                for c in range(NCH):
                    splits.upto(f"G{2 * c}")
                    splits.upto(f"G{2 * c + 1}")
                    if c:
                        chunk_rest(c - 1, i)
                    splits.upto(f"U{2 * c}")
                    splits.upto(f"U{2 * c + 1}")
                    bank = arrived(Group(("u", c), i))
                    dve.wait_ge(esilu_ready, i * NCH + (c + 1))
                    tt(erow[0:SLOTS, :], esilu[0:SLOTS, :], bank[0:SLOTS, :], ALU.mult).then_inc(erow_ready, 1)
                    if c == 1:
                        dve.wait_ge(wpick_turned, i + 1)
                        cand = dve.value_load(items[0:1, bass.ds(i + 1, 1)], min_val=0, max_val=CAND - 1)
                        build_pick(bass.ds(cand, 1))
                        build_wpick(bass.ds(cand, 1))
                    if c:
                        splits.upto(f"D{2 * c - 2}")
                        splits.upto(f"D{2 * c - 1}")
                token_rests("gather", i, 0)
                chunk_rest(NCH - 1, i)
                token_rests("gather", i, 1)
                splits.upto_first(IU + FIRST)
                dve.wait_ge(h_tok_ready, i * 2 * TT + 2 * TT)
                for t in range(2 * TT):
                    bank = arrived(Group(("comb", t), i))
                    h = h_tok[:, t % TT, (t // TT) * 512:(t // TT) * 512 + 512]
                    tt(h, h, bank[:, :], ALU.add).then_inc(h_tok_ready, 1)
            dve.wait_ge(final_rstd, 1)
            dve.wait_ge(row_loaded, 16)
            for t in range(TT):
                stt(out_tile[:, t, :], h_tok[:, t, :], sumsq[:, t:t + 1], g_row, ALU.mult, ALU.mult)\
                    .then_inc(rows_ready, 1)

        @block.gpsimd
        def _(pool):
            chain = [0]

            def link(ins):
                chain[0] += 1
                ins.then_inc(pool_chain, 1)
                pool.wait_ge(pool_chain, chain[0])

            tt, ts = nc.gpsimd.tensor_tensor, nc.gpsimd.tensor_scalar
            link(nc.gpsimd.memset(ident[:, :], 0.0))
            nc.gpsimd.affine_select(out=ident[:, :], in_=ident[:, :], compare_op=ALU.not_equal, fill=1.0, base=0,
                                    pattern=[[-1, P]], channel_multiplier=1).then_inc(consts_made, 1)
            link(nc.gpsimd.memset(neg_incl[:, :], -1.0))
            nc.gpsimd.affine_select(out=neg_incl[:, :], in_=neg_incl[:, :], compare_op=ALU.is_ge, fill=0.0,
                                    base=0, pattern=[[-1, P]], channel_multiplier=1).then_inc(consts_made, 1)
            link(nc.gpsimd.memset(bias[:, 0:1], EPS))
            link(nc.gpsimd.memset(bias[:, 1:2], 1.0))
            link(nc.gpsimd.memset(uconv[:, :, 0:2], 0.0))
            nc.gpsimd.memset(neg_ones[:, :], -1.0).then_inc(consts_made, 1)
            numbers = vtmp[:, 0, 0:SLOTS].bitcast(I32)
            link(nc.gpsimd.iota(numbers, pattern=[[1, SLOTS]], base=0, channel_multiplier=0))
            nc.gpsimd.tensor_copy(slot_no[:, :], numbers).then_inc(consts_made, 1)

            def mask(ready, number, masked):
                pool.wait_ge(ready, number)
                for lo in (0, L):
                    blk = attn[:, :, lo:lo + P]
                    last = nc.gpsimd.affine_select(out=blk, in_=blk, compare_op=ALU.is_gt, fill=0.0,
                                                   base=0, pattern=[[0, HB], [1, P]],
                                                   channel_multiplier=-1)
                    if lo == 0:
                        link(last)
                last.then_inc(masked, 1)

            def ssm_parameters(l):
                if l:
                    pool.wait_ge(states_used, l * SJ)
                    pool.wait_ge(work_done, Group((l - 1, "glu", 0)).done)
                js = slice(l * SJ, l * SJ + SJ)
                for c, (b_src, c_src) in enumerate(((b_re, c_re), (b_im, c_im))):
                    pool.dma_start(braw[:, c, :, :], b_src[l].rearrange("g p h -> (g p) h")
                                   .rearrange("(j s) h -> s j h", s=P)).then_inc(ssm_loaded, 16)
                    pool.dma_start(craw[:, c, :, :], c_src[l].rearrange("g p h -> (g p) h")
                                   .rearrange("(j s) h -> s j h", s=P)).then_inc(ssm_loaded, 16)
                pool.dma_start(wglu[:, :, :], rows(w_glu[l])).then_inc(glu_loaded, 16)
                link(nc.gpsimd.memset(bbp[:, :, :], 0.0))
                link(nc.gpsimd.memset(cblk[:, :, :, :], 0.0))
                pool.wait_ge(ssm_loaded, 64 * (l + 1))
                pool.wait_ge(f_ready, 1)
                fr = f_re[:, js].unsqueeze(2).to_broadcast([P, SJ, GH])
                fi = f_im[:, js].unsqueeze(2).to_broadcast([P, SJ, GH])
                m = [rtmp[:, q, 0:SJ * GH].rearrange("p (j h) -> p j h", h=GH) for q in range(4)]
                link(tt(m[0], braw[:, 0, :, :], fr, ALU.mult))
                link(tt(m[1], braw[:, 1, :, :], fi, ALU.mult))
                link(tt(m[2], braw[:, 1, :, :], fr, ALU.mult))
                link(tt(m[3], braw[:, 0, :, :], fi, ALU.mult))
                for par in range(2):
                    r = slice(par * P // 2, par * P // 2 + P // 2)
                    hs = slice(par * GH, par * GH + GH)
                    for c, op in ((0, ALU.subtract), (1, ALU.add)):
                        dst = bbp[r, c, :].rearrange("p (j h) -> p j h", h=2 * GH)[:, :, hs]
                        link(tt(dst, m[2 * c][r], m[2 * c + 1][r], op))
                    link(ts(cblk[r, 0, :, hs], craw[r, 0, :, :], 1.0, None, ALU.mult))
                    link(ts(cblk[r, 1, :, hs], craw[r, 1, :, :], -1.0, None, ALU.mult))
                nc.gpsimd.memset(cosT[:, :, 0:1], 1.0).then_inc(bbp_ready, 1)
                pc, ps, p2, p3, p4 = [power[:, q, :] for q in range(5)]
                link(nc.gpsimd.memset(sinT[:, :, 0:1], 0.0))
                link(nc.gpsimd.tensor_copy(pc, cos1[:, js]))
                nc.gpsimd.tensor_copy(ps, sin1[:, js]).then_inc(c_ready, 1)
                pool.wait_ge(c_ready, l + 1)
                pool.wait_ge(bbp_ready, l + 1)
                n = 1
                while n < L:
                    if l == 0 and 2 * n == L:
                        mask(stay_ready, 1, stay_masked)
                    old, new = slice(0, n), slice(n, 2 * n)
                    bc = pc.unsqueeze(2).to_broadcast([P, SJ, n])
                    bs = ps.unsqueeze(2).to_broadcast([P, SJ, n])
                    tmp = rtmp[:, :, :].rearrange("p t n -> p (t n)")[:, 0:SJ * n].rearrange("p (j n) -> p j n", n=n)
                    tt(cosT[:, :, new], cosT[:, :, old], bc, ALU.mult)
                    link(tt(tmp, sinT[:, :, old], bs, ALU.mult))
                    tt(sinT[:, :, new], sinT[:, :, old], bc, ALU.mult)
                    link(tt(cosT[:, :, new], cosT[:, :, new], tmp, ALU.subtract))
                    link(tt(tmp, cosT[:, :, old], bs, ALU.mult))
                    last = tt(sinT[:, :, new], sinT[:, :, new], tmp, ALU.add)
                    n *= 2
                    if n == L:
                        last.then_inc(tables_ready, 1)
                        break
                    link(last)
                    link(tt(p2, pc, pc, ALU.mult))
                    link(tt(p3, ps, ps, ALU.mult))
                    link(tt(p4, pc, ps, ALU.mult))
                    link(tt(pc, p2, p3, ALU.subtract))
                    link(tt(ps, p4, p4, ALU.add))

            for l in range(DEPTH):
                ssm_parameters(l)
                for kind, t in STEPS:
                    if kind == "softplus":
                        if (l, t) != (0, 0):
                            mask(stay_ready, 2 * l + t + 1, stay_masked)
                    elif kind == "tail":
                        mask(w_ready, 2 * l + t + 1, w_masked)
                    elif kind == "bu":
                        pool.wait_ge(scanned, 2 * (l * SJ + t + 1))
                        s_re, s_im = sring[:, t % 4, 0, :], sring[:, t % 4, 1, :]
                        tt(rtmp[:, 0, :], s_re, cosT[:, t, :], ALU.mult)
                        tt(rtmp[:, 1, :], s_im, sinT[:, t, :], ALU.mult)
                        tt(rtmp[:, 2, :], s_re, sinT[:, t, :], ALU.mult)
                        link(tt(rtmp[:, 3, :], s_im, cosT[:, t, :], ALU.mult))
                        link(tt(s_re, rtmp[:, 0, :], rtmp[:, 1, :], ALU.subtract))
                        tt(s_im, rtmp[:, 2, :], rtmp[:, 3, :], ALU.add).then_inc(states_ready, 1)
                        pool.wait_ge(states_ready, l * SJ + t + 1)


_NAMES = ["x", "norm_mix", "w_in", "ssm_lambda_re", "ssm_lambda_im", "ssm_log_dt", "ssm_b_re", "ssm_b_im",
          "ssm_c_re", "ssm_c_im", "ssm_d", "ssm_w_glu", "conv_w", "w_br_a", "w_br_b", "w_br_c", "w_out",
          "norm_ffn", "dense_w_gate", "dense_w_up", "dense_w_down", "moe_w_router", "moe_w_gate", "moe_w_up",
          "moe_w_down", "final_norm"]


def _lay_out(inputs):
    import numpy as np

    a = {n: np.asarray(inputs[n]) for n in _NAMES}
    depth, d = a["norm_mix"].shape
    p = 128
    a["x"] = a["x"][0]
    for n in ("norm_mix", "norm_ffn"):
        a[n] = a[n].reshape(depth, d // p, p).transpose(0, 2, 1)
    for n in ("ssm_lambda_re", "ssm_lambda_im"):
        a[n] = a[n].reshape(depth, -1, p).transpose(2, 0, 1)
    a["ssm_log_dt"] = a["ssm_log_dt"].reshape(depth, -1, 2).transpose(2, 0, 1)
    for n in ("ssm_c_re", "ssm_c_im"):
        a[n] = a[n].transpose(0, 1, 3, 2)
    a["ssm_d"] = a["ssm_d"].reshape(depth, -1, p).transpose(2, 0, 1)
    a["conv_w"] = a["conv_w"].reshape(depth, a["conv_w"].shape[1], -1, p).transpose(3, 0, 1, 2)
    a["final_norm"] = a["final_norm"].reshape(1, d)
    return {n: np.ascontiguousarray(v) for n, v in a.items()}


def kernel(**inputs):
    import numpy as _np
    import concourse.bacc as _bacc
    from concourse import mybir as _mybir
    from concourse.bass_utils import run_bass_kernel_spmd as _run

    nc = _bacc.Bacc("TRN2", target_bir_lowering=False, num_devices=1, dynamic_dma_scratch_size=2048)
    arrays, args = {}, []
    for name, a in _lay_out(inputs).items():
        arrays[f"in_{name}"] = a
        args.append(nc.dram_tensor(f"in_{name}", a.shape, _mybir.dt.from_np(a.dtype), kind="ExternalInput").ap())
    shape = arrays["in_x"].shape
    out = nc.dram_tensor("out", shape, _mybir.dt.from_np(_np.dtype("float32")), kind="ExternalOutput").ap()
    trunk_kernel(nc, *args, out)
    r = _run(nc, [arrays], core_ids=[0])
    return r.results[0]["out"].reshape(1, *shape)
```
